# Optimizing a Trainium2 kernel written in Bass

```python
import jax
import jax.numpy as jnp
from jax import lax
import numpy as np

D_MODEL = 1024
BATCH = 1
SEQ = 256
DEPTH = 2

HEAD_DIM = 64
ROPE_THETA = 10000.0
NORM_EPS = 1e-6

MOBA_HEADS = 8
MOBA_BLOCK = 256
MOBA_TOPK = 3
MOBA_Q_CHUNK = 128
MOBA_WIDTH = MOBA_HEADS * HEAD_DIM
RET_HEADS = 4
RET_QK_DIM = 64
RET_V_DIM = 128
RET_CHUNK = 128
RET_THETA = 10000.0
RET_QK_WIDTH = RET_HEADS * RET_QK_DIM
RET_V_WIDTH = RET_HEADS * RET_V_DIM
EVEN_IN_WIDTH = 3 * MOBA_WIDTH + 2 * RET_QK_WIDTH + 2 * RET_V_WIDTH
EVEN_MIX_WIDTH = MOBA_WIDTH + RET_V_WIDTH

DIL_HEADS = D_MODEL // HEAD_DIM
DIL_PATTERNS = ((128, 1), (512, 4), (2048, 16))
DIL_BLOCK = 128
ODD_IN_WIDTH = 3 * DIL_HEADS * HEAD_DIM
ODD_MIX_WIDTH = DIL_HEADS * HEAD_DIM

MOE_GROUPS = 4
MOE_EXPERTS_PER_GROUP = 8
MOE_EXPERTS = MOE_GROUPS * MOE_EXPERTS_PER_GROUP
MOE_TOPK = 2
MOE_HIDDEN = D_MODEL // 2
MOE_ROW_BLOCK = 128

kernel_name = 'hybrid_moba_retnet_dilated_hmoe'

def rms_norm(x, gain):
    xf = x.astype(jnp.float32)
    y = xf * lax.rsqrt(jnp.mean(xf * xf, axis=-1, keepdims=True) + NORM_EPS)
    return (y * gain.astype(jnp.float32)).astype(x.dtype)

def split_heads(t, n_heads):
    b, s, _ = t.shape
    return t.reshape(b, s, n_heads, -1).transpose(0, 2, 1, 3)

def merge_heads(t):
    b, h, s, d = t.shape
    return t.transpose(0, 2, 1, 3).reshape(b, s, h * d)

def rotary(x):
    s, dh = x.shape[2], x.shape[3]
    half = dh // 2
    inv_freq = 1.0 / (ROPE_THETA ** (jnp.arange(half, dtype=jnp.float32) * (2.0 / dh)))
    ang = jnp.arange(s, dtype=jnp.float32)[:, None] * inv_freq[None, :]
    cos, sin = jnp.cos(ang), jnp.sin(ang)
    xf = x.astype(jnp.float32)
    x1, x2 = xf[..., :half], xf[..., half:]
    return jnp.concatenate([x1 * cos - x2 * sin, x1 * sin + x2 * cos], axis=-1).astype(x.dtype)

def retnet_rotation(x):
    s, dk = x.shape[2], x.shape[3]
    half = dk // 2
    freq = 1.0 / (RET_THETA ** jnp.linspace(0.0, 1.0, half, dtype=jnp.float32))
    ang = jnp.arange(s, dtype=jnp.float32)[:, None] * freq[None, :]
    cos, sin = jnp.cos(ang), jnp.sin(ang)
    xf = x.astype(jnp.float32).reshape(x.shape[:-1] + (half, 2))
    xe, xo = xf[..., 0], xf[..., 1]
    out = jnp.stack([xe * cos - xo * sin, xe * sin + xo * cos], axis=-1)
    return out.reshape(x.shape).astype(x.dtype)

def moba_attention(q, k, v):
    b, h, s, dh = q.shape
    n_blk = -(-s // MOBA_BLOCK)
    sp = n_blk * MOBA_BLOCK
    pad = ((0, 0), (0, 0), (0, sp - s), (0, 0))
    q, k, v = jnp.pad(q, pad), jnp.pad(k, pad), jnp.pad(v, pad)
    scale = dh ** -0.5
    k_blocks = k.reshape(b, h, n_blk, MOBA_BLOCK, dh)
    v_blocks = v.reshape(b, h, n_blk, MOBA_BLOCK, dh)
    k_mean = k_blocks.astype(jnp.float32).mean(axis=3).astype(q.dtype)
    gate = jnp.einsum('bhsd,bhnd->bhsn', q, k_mean).astype(jnp.float32)
    q_blk = jnp.arange(sp) // MOBA_BLOCK
    fully_past = jnp.arange(n_blk)[None, :] < q_blk[:, None]
    gate = jnp.where(fully_past, gate, -jnp.inf)
    n_sel = min(MOBA_TOPK, n_blk)
    _, sel = lax.top_k(gate, n_sel)
    sel_ok = sel < q_blk[:, None]
    bi = jnp.arange(b)[:, None, None, None]
    hi = jnp.arange(h)[None, :, None, None]
    n_chunk = sp // MOBA_Q_CHUNK

    def chunk(c):
        q0 = c * MOBA_Q_CHUNK
        blk = q0 // MOBA_BLOCK
        qc = lax.dynamic_slice_in_dim(q, q0, MOBA_Q_CHUNK, axis=2)
        k_own = lax.dynamic_slice_in_dim(k, blk * MOBA_BLOCK, MOBA_BLOCK, axis=2)
        v_own = lax.dynamic_slice_in_dim(v, blk * MOBA_BLOCK, MOBA_BLOCK, axis=2)
        sel_c = lax.dynamic_slice_in_dim(sel, q0, MOBA_Q_CHUNK, axis=2)
        ok_c = lax.dynamic_slice_in_dim(sel_ok, q0, MOBA_Q_CHUNK, axis=2)
        k_sel = k_blocks[bi, hi, sel_c]
        v_sel = v_blocks[bi, hi, sel_c]
        qpos = q0 + jnp.arange(MOBA_Q_CHUNK)
        kpos = blk * MOBA_BLOCK + jnp.arange(MOBA_BLOCK)
        s_own = jnp.einsum('bhqd,bhkd->bhqk', qc, k_own).astype(jnp.float32) * scale
        s_own = jnp.where(kpos[None, :] <= qpos[:, None], s_own, -jnp.inf)
        s_sel = jnp.einsum('bhqd,bhqnkd->bhqnk', qc, k_sel).astype(jnp.float32) * scale
        s_sel = jnp.where(ok_c[..., None], s_sel, -jnp.inf)
        s_all = jnp.concatenate([s_own, s_sel.reshape(b, h, MOBA_Q_CHUNK, n_sel * MOBA_BLOCK)], axis=-1)
        p = jax.nn.softmax(s_all, axis=-1).astype(v.dtype)
        p_own = p[..., :MOBA_BLOCK]
        p_sel = p[..., MOBA_BLOCK:].reshape(b, h, MOBA_Q_CHUNK, n_sel, MOBA_BLOCK)
        return (jnp.einsum('bhqk,bhkd->bhqd', p_own, v_own)
                + jnp.einsum('bhqnk,bhqnkd->bhqd', p_sel, v_sel))

    out = lax.map(chunk, jnp.arange(n_chunk))
    return out.transpose(1, 2, 0, 3, 4).reshape(b, h, sp, dh)[:, :, :s]

def retention(q, k, v):
    b, h, s, dk = q.shape
    dv = v.shape[-1]
    c = RET_CHUNK
    n = s // c
    log_gamma = jnp.log(1.0 - 2.0 ** (-5.0 - jnp.arange(h, dtype=jnp.float32)))
    qf = q.astype(jnp.float32).reshape(b, h, n, c, dk)
    kf = k.astype(jnp.float32).reshape(b, h, n, c, dk) * (dk ** -0.5)
    vf = v.astype(jnp.float32).reshape(b, h, n, c, dv)
    pos = jnp.arange(c, dtype=jnp.float32)
    rel = pos[:, None] - pos[None, :]
    decay = jnp.where(rel >= 0, jnp.exp(log_gamma[:, None, None] * jnp.maximum(rel, 0.0)), 0.0)
    scores = jnp.einsum('bhnid,bhnjd->bhnij', qf, kf) * decay[None, :, None]
    intra = jnp.einsum('bhnij,bhnje->bhnie', scores, vf)
    k_tail = kf * jnp.exp(log_gamma[:, None] * (c - 1.0 - pos))[None, :, None, :, None]
    chunk_state = jnp.einsum('bhnjd,bhnje->nbhde', k_tail, vf)
    gamma_c = jnp.exp(log_gamma * c)[None, :, None, None]

    def step(r, u):
        return gamma_c * r + u, r

    _, r_prev = lax.scan(step, jnp.zeros((b, h, dk, dv), jnp.float32), chunk_state)
    q_head = qf * jnp.exp(log_gamma[:, None] * (pos + 1.0))[None, :, None, :, None]
    inter = jnp.einsum('bhnid,nbhde->bhnie', q_head, r_prev)
    y = (intra + inter).reshape(b, h, s, dv)
    mu = jnp.mean(y, axis=-1, keepdims=True)
    var = jnp.mean(jnp.square(y - mu), axis=-1, keepdims=True)
    return ((y - mu) * lax.rsqrt(var + NORM_EPS)).astype(v.dtype)

def dilated_branch(q, k, v, window, dil):
    b, h, s, dh = q.shape
    w_d = window // dil
    blk = DIL_BLOCK
    n_blk = -(-s // (dil * blk))
    length = n_blk * blk
    sp = length * dil
    pad = ((0, 0), (0, 0), (0, sp - s), (0, 0))
    q, k, v = jnp.pad(q, pad), jnp.pad(k, pad), jnp.pad(v, pad)

    def decimate(t):
        return t.reshape(b, h, length, dil, dh).transpose(0, 1, 3, 2, 4).reshape(b, h, dil, n_blk, blk, dh)

    def with_prev(t):
        prev = jnp.concatenate([jnp.zeros_like(t[:, :, :, :1]), t[:, :, :, :-1]], axis=3)
        return jnp.concatenate([prev, t], axis=4)

    qd = decimate(q)
    kc = with_prev(decimate(k))
    vc = with_prev(decimate(v))
    a = jnp.arange(blk)[:, None]
    e = jnp.arange(2 * blk)[None, :]
    dist = blk + a - e
    band = (dist >= 0) & (dist <= w_d)
    not_before_start = (jnp.arange(n_blk)[:, None, None] > 0) | (e >= blk)[None]
    mask = band[None] & not_before_start
    sc = jnp.einsum('bhrnqd,bhrnkd->bhrnqk', qd, kc).astype(jnp.float32) * (dh ** -0.5)
    sc = jnp.where(mask, sc, -jnp.inf)
    m = jnp.max(sc, axis=-1, keepdims=True)
    p = jnp.exp(sc - m)
    den = jnp.sum(p, axis=-1, keepdims=True)
    o = jnp.einsum('bhrnqk,bhrnkd->bhrnqd', (p / den).astype(v.dtype), vc)
    lse = (m + jnp.log(den))[..., 0]
    o = o.reshape(b, h, dil, length, dh).transpose(0, 1, 3, 2, 4).reshape(b, h, sp, dh)[:, :, :s]
    lse = lse.reshape(b, h, dil, length).transpose(0, 1, 3, 2).reshape(b, h, sp)[:, :, :s]
    return o, lse

def dilated_mixture(q, k, v):
    branches = [dilated_branch(q, k, v, w, d) for (w, d) in DIL_PATTERNS]
    lses = jnp.stack([l for (_, l) in branches], axis=0)
    wts = jax.nn.softmax(lses, axis=0)
    out = wts[0][..., None] * branches[0][0].astype(jnp.float32)
    for i in range(1, len(branches)):
        out = out + wts[i][..., None] * branches[i][0].astype(jnp.float32)
    return out.astype(q.dtype)

def even_mixer(h, w_in, w_out):
    proj = h @ w_in
    s1 = MOBA_WIDTH
    s2 = 2 * MOBA_WIDTH
    s3 = 3 * MOBA_WIDTH
    s4 = s3 + RET_QK_WIDTH
    s5 = s4 + RET_QK_WIDTH
    s6 = s5 + RET_V_WIDTH
    aq, ak, av, rq, rk, rv, rg = jnp.split(proj, [s1, s2, s3, s4, s5, s6], axis=-1)
    a_out = moba_attention(rotary(split_heads(aq, MOBA_HEADS)),
                           rotary(split_heads(ak, MOBA_HEADS)),
                           split_heads(av, MOBA_HEADS))
    r_out = retention(retnet_rotation(split_heads(rq, RET_HEADS)),
                      retnet_rotation(split_heads(rk, RET_HEADS)),
                      split_heads(rv, RET_HEADS))
    r_out = merge_heads(r_out) * jax.nn.silu(rg)
    return jnp.concatenate([merge_heads(a_out), r_out], axis=-1) @ w_out

def odd_mixer(h, w_in, w_out):
    q, k, v = jnp.split(h @ w_in, 3, axis=-1)
    o = dilated_mixture(rotary(split_heads(q, DIL_HEADS)),
                        rotary(split_heads(k, DIL_HEADS)),
                        split_heads(v, DIL_HEADS))
    return merge_heads(o) @ w_out

def hier_moe(h, w_group, b_group, w_fine, b_fine, w_gate, w_up, w_down):
    b, s, d = h.shape
    n_tok = b * s
    x2 = h.reshape(n_tok, d)
    g_logits = (x2 @ w_group).astype(jnp.float32) + b_group.astype(jnp.float32)
    g_prob = jax.nn.softmax(g_logits, axis=-1)
    g_val, grp = lax.top_k(g_prob, 1)
    f_logits = ((x2 @ w_fine).astype(jnp.float32) + b_fine.astype(jnp.float32)).reshape(
        n_tok, MOE_GROUPS, MOE_EXPERTS_PER_GROUP)
    f_in_group = jnp.take_along_axis(f_logits, grp[:, :, None], axis=1)[:, 0]
    top_v, top_i = lax.top_k(f_in_group, MOE_TOPK)
    gates = g_val * jax.nn.softmax(top_v, axis=-1)
    expert = grp * MOE_EXPERTS_PER_GROUP + top_i
    n_assign = n_tok * MOE_TOPK
    e_flat = expert.reshape(-1)
    t_flat = jnp.repeat(jnp.arange(n_tok, dtype=jnp.int32), MOE_TOPK)
    g_flat = gates.reshape(-1)
    order = jnp.argsort(e_flat)
    e_s, t_s, g_s = e_flat[order], t_flat[order], g_flat[order]
    counts = jnp.bincount(e_flat, length=MOE_EXPERTS)
    starts = jnp.cumsum(counts) - counts
    padded = ((counts + MOE_ROW_BLOCK - 1) // MOE_ROW_BLOCK) * MOE_ROW_BLOCK
    p_ends = jnp.cumsum(padded)
    p_starts = p_ends - padded
    dest = p_starts[e_s] + (jnp.arange(n_assign) - starts[e_s])
    n_blocks = -(-n_assign // MOE_ROW_BLOCK) + MOE_EXPERTS
    n_rows = n_blocks * MOE_ROW_BLOCK
    row_tok = jnp.zeros((n_rows,), jnp.int32).at[dest].set(t_s)
    row_gate = jnp.zeros((n_rows,), jnp.float32).at[dest].set(g_s)
    blk_start = jnp.arange(n_blocks) * MOE_ROW_BLOCK
    blk_exp = jnp.minimum(jnp.searchsorted(p_ends, blk_start, side='right'), MOE_EXPERTS - 1)

    def expert_block(args):
        tok, e = args
        xb = x2[tok]
        hid = jax.nn.silu(xb @ w_gate[e]) * (xb @ w_up[e])
        return hid @ w_down[e]

    ys = lax.map(expert_block, (row_tok.reshape(n_blocks, MOE_ROW_BLOCK), blk_exp)).reshape(n_rows, d)
    out = jnp.zeros((n_tok, d), jnp.float32).at[row_tok].add(ys.astype(jnp.float32) * row_gate[:, None])
    return out.astype(h.dtype).reshape(b, s, d)

def setup_inputs(seed: int = 0) -> dict:
    key = jax.random.key(seed)
    ks = jax.random.split(key, 17)
    n_even = (DEPTH + 1) // 2
    n_odd = DEPTH // 2

    def dense(k, shape, fan_in):
        return jax.random.normal(k, shape, jnp.float32) * (fan_in ** -0.5)

    def gain(k, shape):
        return 1.0 + 0.02 * jax.random.normal(k, shape, jnp.float32)

    return {
        'x': jax.random.normal(ks[0], (BATCH, SEQ, D_MODEL), jnp.float32),
        'mix_norm_even': gain(ks[1], (n_even, D_MODEL)),
        'w_in_even': dense(ks[2], (n_even, D_MODEL, EVEN_IN_WIDTH), D_MODEL),
        'w_out_even': dense(ks[3], (n_even, EVEN_MIX_WIDTH, D_MODEL), EVEN_MIX_WIDTH),
        'mix_norm_odd': gain(ks[4], (n_odd, D_MODEL)),
        'w_in_odd': dense(ks[5], (n_odd, D_MODEL, ODD_IN_WIDTH), D_MODEL),
        'w_out_odd': dense(ks[6], (n_odd, ODD_MIX_WIDTH, D_MODEL), ODD_MIX_WIDTH),
        'ffn_norm': gain(ks[7], (DEPTH, D_MODEL)),
        'w_router_group': dense(ks[8], (DEPTH, D_MODEL, MOE_GROUPS), D_MODEL),
        'b_router_group': 0.01 * jax.random.normal(ks[9], (DEPTH, MOE_GROUPS), jnp.float32),
        'w_router_expert': dense(ks[10], (DEPTH, D_MODEL, MOE_EXPERTS), D_MODEL),
        'b_router_expert': 0.01 * jax.random.normal(ks[11], (DEPTH, MOE_EXPERTS), jnp.float32),
        'w_expert_gate': dense(ks[12], (DEPTH, MOE_EXPERTS, D_MODEL, MOE_HIDDEN), D_MODEL),
        'w_expert_up': dense(ks[13], (DEPTH, MOE_EXPERTS, D_MODEL, MOE_HIDDEN), D_MODEL),
        'w_expert_down': dense(ks[14], (DEPTH, MOE_EXPERTS, MOE_HIDDEN, D_MODEL), MOE_HIDDEN),
        'final_norm': gain(ks[15], (D_MODEL,)),
    }

def reference(x, mix_norm_even, w_in_even, w_out_even, mix_norm_odd, w_in_odd, w_out_odd,
              ffn_norm, w_router_group, b_router_group, w_router_expert, b_router_expert,
              w_expert_gate, w_expert_up, w_expert_down, final_norm):
    h = x
    for layer in range(DEPTH):
        i = layer // 2
        if layer % 2 == 0:
            h = h + even_mixer(rms_norm(h, mix_norm_even[i]), w_in_even[i], w_out_even[i])
        else:
            h = h + odd_mixer(rms_norm(h, mix_norm_odd[i]), w_in_odd[i], w_out_odd[i])
        h = h + hier_moe(rms_norm(h, ffn_norm[layer]), w_router_group[layer], b_router_group[layer],
                         w_router_expert[layer], b_router_expert[layer], w_expert_gate[layer],
                         w_expert_up[layer], w_expert_down[layer])
    return rms_norm(h, final_norm)


_drawn_inputs = setup_inputs


def setup_inputs(seed=0):
    import zlib

    import numpy as np

    out = dict(_drawn_inputs(seed))
    spreads = {}
    factors = {'mix_norm_odd': 2.889,
     'b_router_group': 3.303,
     'b_router_expert': 3.07,
     'final_norm': 2.862}
    for name, (base, spread) in spreads.items():
        noise = np.random.default_rng([zlib.crc32(name.encode()), seed]).standard_normal(out[name].shape)
        drawn = base * np.exp(spread * noise) if base else spread * noise
        out[name] = jnp.asarray(drawn.astype(out[name].dtype))
    for name, factor in factors.items():
        out[name] = (out[name] * factor).astype(out[name].dtype)
    return out
```

```python
from contextlib import ExitStack

import numpy as np

import concourse.bass as bass
from concourse import mybir

F32 = mybir.dt.float32
I32 = mybir.dt.int32
U32 = mybir.dt.uint32
ALU = mybir.AluOpType
ACT = mybir.ActivationFunctionType
AX = mybir.AxisListType

P = 128
D = 1024
SEQ = 256
T = SEQ // P
C = D // P
LAYERS = 2
HEAD = 64
NW = 6
HEADS = (8, 16)
RET = 4
ROTATED = (3, 4)
BLOCKS = ((0, 1, 3, 2, 4, 5), (0, 1, 2, 3, 4, 5))
EXPERTS = 32
GROUPS = 4
SLOTS = 32
GE = 3
FULL = EXPERTS // GE
TAIL = EXPERTS - FULL * GE
HID = 512
MAX_ROUNDS = SEQ // SLOTS
EPS = 1e-6
FAR = 3.0e38
UNIT = 4096

CONST_WIDTHS = (
    ("ident", P), ("before", P), ("ones", P), ("iota", 32), ("limits", 8),
    ("mask0", 3 * P), ("mask1", 3 * P), ("count1", 3 * P),
    ("rope_cos", T * HEAD), ("rope_sin", T * HEAD), ("ret_cos", T * HEAD), ("ret_sin", T * HEAD),
    ("decay", RET * 2 * P),
)
CONST_AT = {}
_at = 0
for _name, _w in CONST_WIDTHS:
    CONST_AT[_name] = (_at, _w)
    _at += _w
CONST_COLS = _at


def shape_constants():
    f = np.float32
    out = np.zeros((P, CONST_COLS), f)

    def put(name, a):
        at, w = CONST_AT[name]
        out[:, at:at + w] = np.asarray(a, f).reshape(P, w)

    i = np.arange(P)
    put("ident", np.eye(P))
    put("before", i[:, None] < i[None, :])
    put("ones", np.ones((P, P)))
    put("iota", np.tile(np.arange(32), (P, 1)))
    put("limits", np.tile(np.arange(8) * SLOTS, (P, 1)))
    q, k = i[:, None], i[None, :]
    causal = np.where(k <= q, 0.0, -1e30)
    put("mask0", np.concatenate([causal, np.zeros((P, P)), causal], 1))

    def windows(dist):
        n = np.zeros(dist.shape)
        for window, dil in ((128, 1), (512, 4), (2048, 16)):
            n += (dist >= 0) & (dist % dil == 0) & (dist // dil <= window // dil)
        return n

    near, far = windows(q - k), windows(q + P - k)
    count = np.concatenate([near, far, near], 1)
    put("count1", count)
    put("mask1", np.where(count > 0, 0.0, -1e30))
    half = HEAD // 2
    pos = np.arange(SEQ, dtype=f)[:, None]
    inv = (f(1.0) / (f(10000.0) ** (np.arange(half, dtype=f) * f(2.0 / HEAD)))).astype(f)
    ang = pos * inv[None, :]
    cos, sin = np.cos(ang).astype(f), np.sin(ang).astype(f)
    tok = lambda a: a.reshape(T, P, -1).transpose(1, 0, 2)
    put("rope_cos", tok(np.concatenate([cos, cos], 1)))
    put("rope_sin", tok(np.concatenate([-sin, sin], 1)))
    freq = (f(1.0) / (f(10000.0) ** np.linspace(0.0, 1.0, half, dtype=f))).astype(f)
    ang = pos * freq[None, :]
    cos, sin = np.cos(ang).astype(f), np.sin(ang).astype(f)
    put("ret_cos", tok(np.stack([cos, cos], -1).reshape(SEQ, HEAD)))
    put("ret_sin", tok(np.stack([-sin, sin], -1).reshape(SEQ, HEAD)))
    rel = np.arange(SEQ)[None, :] - i[:, None]
    decay = []
    for h in range(RET):
        log_gamma = np.log(1.0 - 2.0 ** (-5.0 - h))
        decay.append(np.where(rel >= 0, np.exp(log_gamma * np.maximum(rel, 0)), 0.0) * HEAD ** -0.5)
    put("decay", np.stack(decay, 1))
    return out


class Chain:

    def __init__(self, eng, sem, base=0):
        self.eng, self.sem, self.base, self.n = eng, sem, base, 0

    def link(self, ins):
        self.n += 1
        ins.then_inc(self.sem, 1)
        self.eng.wait_ge(self.sem, self.base + self.n)


def group_no(r, g):
    return r * (FULL + 1) + g


def expert_no(r, g, k):
    return r * EXPERTS + g * GE + k


def gu_count(r, g, k):
    return r * ((FULL + 1) * GE) + g * GE + (k + 1)


def arrivals(pos, r, g):
    per_round = FULL if pos in (4, 5, 8) else FULL + 1
    return (r * per_round + g + 1) * 16


DVE_GROUP = 1 + 3 * GE
DVE_ROUND = FULL * DVE_GROUP + 1 + 3 * TAIL + 1


def build(nc, x, mix_even, w_in_even, w_out_even, mix_odd, w_in_odd, w_out_odd, ffn_norm,
          w_group, b_group, w_fine, b_fine, w_gate, w_up, w_down, final_norm, consts, out):
    w_in = (w_in_even, w_in_odd)
    w_out = (w_out_even, w_out_odd)
    mix = (mix_even, mix_odd)
    with ExitStack() as ctx:
        def sb(name, shape, dt=F32):
            return ctx.enter_context(nc.sbuf_tensor(name, shape, dt))

        def sem(name):
            return ctx.enter_context(nc.semaphore(name))

        def sems(name, n):
            return [sem(f"{name}{i}") for i in range(n)]

        ring = sb("ring", [P, 9, UNIT])
        h = sb("h", [P, T, D])
        xn = sb("xn", [P, T * D])
        xnT = sb("xnT", [P, C, SEQ])
        work = sb("work", [P, 5632])
        cst = sb("cst", [P, CONST_COLS])
        gains = sb("gains", [P, 2 * LAYERS, C])
        w_rt = sb("w_rt", [P, LAYERS, C, GROUPS + EXPERTS])
        b_rt = sb("b_rt", [P, LAYERS, GROUPS + EXPERTS])
        small = sb("small", [P, 320])
        idx_u = sb("idx_u", [P, 2 * T, 8], U32)
        rounds_i = sb("rounds_i", [P, LAYERS], I32)
        psum = [ctx.enter_context(nc.psum_tensor(f"bank{i}", [P, 512], F32)) for i in range(8)]

        def const(name, *shape):
            at, w = CONST_AT[name]
            v = cst[:, at:at + w]
            if len(shape) == 2:
                v = v.rearrange("p (a b) -> p a b", a=shape[0])
            return v

        ident = const("ident")
        xn_t = xn[:, :].rearrange("p (t d) -> p t d", t=T)
        xn_c = xn[:, :].rearrange("p (t c q) -> p t c q", t=T, c=C)
        rot = [xn[:, 512 * i:512 * i + 512] for i in range(3)]
        rot_tmp = xn[:, 1536:2048]
        o_sb = xn_t
        oT = xnT
        qT = ring[:, 8, 0:2048].rearrange("p (a s) -> p a s", a=8)
        kT = ring[:, 8, 2048:4096].rearrange("p (a s) -> p a s", a=8)
        v_sb = work[:, 0:2048].rearrange("p (t d) -> p t d", t=T)
        rg = work[:, 2048:3072].rearrange("p (t d) -> p t d", t=T)
        prob = [work[:, 3072 + 384 * i:3072 + 384 * i + 384] for i in range(3)]
        probT = [work[:, 4224 + 384 * i:4224 + 384 * i + 384] for i in range(2)]
        onehot = work[:, 0:192].rearrange("p (t k s) -> p t k s", t=T, k=GE)
        gated = work[:, 192:384].rearrange("p (t k s) -> p t k s", t=T, k=GE)
        gatedT = work[:, 384:640]
        xT = work[:, 640:1408].rearrange("p (c s) -> p c s", c=C)
        eg = [work[:, 1408 + 128 * i:1536 + 128 * i] for i in range(2)]
        gu = [work[:, 1664 + 256 * i:1920 + 256 * i] for i in range(2)]
        hid = [work[:, 2176 + 128 * i:2304 + 128 * i] for i in range(2)]
        hidT = [work[:, 2432 + 128 * i:2560 + 128 * i] for i in range(GE)]
        y_sb = work[:, 2816:3840]
        masked = work[:, 3840:3904].rearrange("p (t e) -> p t e", t=T)
        first = work[:, 3904:3968].rearrange("p (t e) -> p t e", t=T)
        second = work[:, 3968:4032].rearrange("p (t e) -> p t e", t=T)
        lf = work[:, 4032:4096].rearrange("p (t e) -> p t e", t=T)
        gain_row = work[:, 4096:5120]
        sumsq, var, rstd, newt = (small[:, 2 * i:2 * i + 2] for i in range(4))
        den = small[:, 8:40].rearrange("p (h t) -> p t h", t=T)
        rden = small[:, 40:72].rearrange("p (h t) -> p t h", t=T)
        mx = small[:, 72:104].rearrange("p (h t) -> p h t", t=T)
        negm = small[:, 104:136].rearrange("p (h t) -> p h t", t=T)
        lg = small[:, 136:152].rearrange("p (t e) -> p t e", t=T)
        top = small[:, 152:184].rearrange("p (a e) -> p a e", a=2 * T)
        idx = small[:, 184:192]
        gv = small[:, 192:208]
        pen = small[:, 208:216].rearrange("p (t e) -> p t e", t=T)
        gmask = small[:, 216:224].rearrange("p (t e) -> p t e", t=T)
        rstat = small[:, 224:240].rearrange("p (t h m) -> p t h m", t=T, h=RET)
        rvar = small[:, 240:248]
        rrstd = small[:, 248:256]
        rounds_f = small[:, 256:258]
        bnst = small[:, 258:306].rearrange("p (a s) -> p a s", a=2 * RET)
        expg = small[:, 306:314].rearrange("p (t e) -> p t e", t=T)
        half_exp = small[:, 314:316]
        cnt = small[:, 316:318]
        posm = sb("posm", [P, T, 36])
        gate = sb("gate", [P, T, 36])
        asg = sb("asg", [P, T, EXPERTS])
        limhit = sb("limhit", [P, MAX_ROUNDS])

        c_loaded = sems("c_loaded", 3)
        w_arrived = [sems(f"w_arrived{l}_", 8) for l in range(LAYERS)]
        e_arrived = [sems(f"e_arrived{l}_", 9) for l in range(LAYERS)]
        fin_loaded = sem("fin_loaded")
        out_stored = sem("out_stored")
        var_ready = sem("var_ready")
        pow_ready = sem("pow_ready")
        xn_ready = sem("xn_ready")
        xn_turned = sem("xn_turned")
        xnT_ready = sem("xnT_ready")
        dve_norm = sem("dve_norm")
        proj_done = sems("proj_done", LAYERS)
        bank_out = [sems(f"bank_out{l}_", 4) for l in range(LAYERS)]
        rot_ready = sems("rot_ready", LAYERS)
        rot_turned = sems("rot_turned", LAYERS)
        qkT_ready = sems("qkT_ready", LAYERS)
        rg_exp = sem("rg_exp")
        s_done = sems("s_done", LAYERS)
        s_out = sems("s_out", LAYERS)
        negm_ready = sems("negm_ready", LAYERS)
        exp_done = sems("exp_done", LAYERS)
        p_ready = sems("p_ready", LAYERS)
        ret_ready = sem("ret_ready")
        p_turned = sems("p_turned", LAYERS)
        pT_ready = sems("pT_ready", LAYERS)
        pv_done = sems("pv_done", LAYERS)
        ret_var = sem("ret_var")
        ret_pow = sem("ret_pow")
        o_ready = sems("o_ready", LAYERS)
        o_turned = sems("o_turned", LAYERS)
        oT_ready = sems("oT_ready", LAYERS)
        mixed = sems("mixed", LAYERS)
        mix_added = sems("mix_added", LAYERS)
        dve_attn = sems("dve_attn", LAYERS)
        logits_done = sems("logits_done", LAYERS)
        gmax_ready = sems("gmax_ready", LAYERS)
        gexp_done = sems("gexp_done", LAYERS)
        assigned = sems("assigned", LAYERS)
        pos_done = sems("pos_done", LAYERS)
        rounds_ready = sems("rounds_ready", LAYERS)
        dve_route = sems("dve_route", LAYERS)
        onehot_ready = sems("onehot_ready", LAYERS)
        gated_turned = sems("gated_turned", LAYERS)
        gatedT_ready = sems("gatedT_ready", LAYERS)
        gathered = sems("gathered", LAYERS)
        xT_ready = sems("xT_ready", LAYERS)
        gate_up_done = sems("gate_up_done", LAYERS)
        gate_up_out = sems("gate_up_out", LAYERS)
        hid_ready = sems("hid_ready", LAYERS)
        hid_turned = sems("hid_turned", LAYERS)
        hidT_ready = sems("hidT_ready", LAYERS)
        down_done = sems("down_done", LAYERS)
        y_low = sems("y_low", LAYERS)
        y_high = sems("y_high", LAYERS)
        scattered = sems("scattered", LAYERS)
        added = sems("added", LAYERS)
        dve_moe = sems("dve_moe", LAYERS)

        n_items = [HEADS[0] + RET, HEADS[1]]
        n_rot = [ROTATED[l] * T for l in range(LAYERS)]

        block = ctx.enter_context(nc.Block())

        @block.sync
        def _(sp):
            gate_rows = w_gate.rearrange("l e (p c) n -> (l e) p (c n)", c=C)
            up_rows = w_up.rearrange("l e (p c) n -> (l e) p (c n)", c=C)
            down_rows = w_down.rearrange("l e (j p) n -> (l e) p j n", p=P)

            def load_group(l, r, g, experts, first_expert, after_attention=False):
                for k in range(experts):
                    if after_attention:
                        sp.wait_ge(proj_done[l], 2 * T * (k + 1))
                    else:
                        sp.wait_ge(gate_up_done[l], gu_count(r, g, k) - GE)
                    row = l * EXPERTS + first_expert + k
                    sp.dma_start(ring[:, 2 * k, :], gate_rows[row]).then_inc(e_arrived[l][2 * k], 16)
                    sp.dma_start(ring[:, 2 * k + 1, :], up_rows[row]).then_inc(e_arrived[l][2 * k + 1], 16)
                if after_attention:
                    sp.wait_ge(mixed[l], 2 * T)
                else:
                    sp.wait_ge(down_done[l], group_no(r, g))
                for k in range(experts):
                    row = l * EXPERTS + first_expert + k
                    sp.dma_start(ring[:, 6 + k, :].rearrange("p (j n) -> p j n", j=HID // P),
                                 down_rows[row]).then_inc(e_arrived[l][6 + k], 16)

            def load_round(l, r, after_attention=False):
                if after_attention:
                    load_group(l, r, 0, GE, 0, after_attention)
                with sp.Fori(int(after_attention), FULL) as g:
                    load_group(l, r, g, GE, g * GE)
                load_group(l, r, FULL, TAIL, FULL * GE)

            more = None
            for l in range(LAYERS):
                w_in_v = w_in[l][0].rearrange("(p c) n -> p c n", c=C)
                w_out_v = w_out[l][0].rearrange("(c p) n -> p c n", p=P)
                for j in range(NW):
                    if l:
                        sp.wait_ge(gate_up_done[l - 1],
                                   gu_count(more, FULL, j // 2))
                    b = BLOCKS[l][j]
                    sp.dma_start(ring[:, j, :].rearrange("p (c n) -> p c n", c=C),
                                 w_in_v[:, :, 512 * b:512 * b + 512]).then_inc(w_arrived[l][j], 16)
                if l:
                    sp.wait_ge(down_done[l - 1], group_no(more, FULL) + 1)
                for n in range(2):
                    sp.dma_start(ring[:, 6 + n, :].rearrange("p (c n) -> p c n", c=C),
                                 w_out_v[:, :, 512 * n:512 * n + 512]).then_inc(w_arrived[l][6 + n], 16)
                load_round(l, 0, after_attention=True)
                sp.wait_ge(rounds_ready[l], 1)
                more = sp.value_load(rounds_i[0:1, l:l + 1], min_val=0, max_val=MAX_ROUNDS - 1)
                with sp.If(more > 0):
                    with sp.Fori(1, more + 1) as r:
                        load_round(l, r)
            sp.wait_ge(xn_ready, 4 * T + T)
            sp.dma_start(out[0].rearrange("(t p) d -> p t d", p=P), xn_t).then_inc(out_stored, 16)
            sp.wait_ge(out_stored, 16)

        @block.gpsimd
        def _(pool):
            pool.memset(half_exp, -0.5).then_inc(pow_ready, 1)
            pool.wait_ge(pow_ready, 1)

            def rsqrt_norm(ph):
                pool.wait_ge(var_ready, ph + 1)
                pool.tensor_tensor(rstd, var, half_exp, ALU.pow).then_inc(pow_ready, 1)

            for l in range(LAYERS):
                rsqrt_norm(2 * l)
                if l == 0:
                    pool.wait_ge(ret_var, 1)
                    pool.tensor_tensor(rrstd, rvar, half_exp[:, 0:1].broadcast_to([P, 8]),
                                       ALU.pow).then_inc(ret_pow, 1)
                rsqrt_norm(2 * l + 1)
            rsqrt_norm(2 * LAYERS)

        @block.scalar
        def _(act):
            act.dma_start(h[:], x[0].rearrange("(t p) d -> p t d", p=P)).then_inc(c_loaded[1], 16)
            act.dma_start(cst[:], consts).then_inc(c_loaded[0], 16)
            for l in range(LAYERS):
                act.dma_start(gains[:, 2 * l, :], mix[l][0].rearrange("(p c) -> p c", c=C)).then_inc(c_loaded[2], 16)
                act.dma_start(gains[:, 2 * l + 1, :], ffn_norm[l].rearrange("(p c) -> p c", c=C)).then_inc(c_loaded[2], 16)
                act.dma_start(w_rt[:, l, :, 0:GROUPS], w_group[l].rearrange("(p c) e -> p c e", c=C)).then_inc(c_loaded[2], 16)
                act.dma_start(w_rt[:, l, :, GROUPS:], w_fine[l].rearrange("(p c) e -> p c e", c=C)).then_inc(c_loaded[2], 16)
                act.dma_start(b_rt[:, l, 0:GROUPS], b_group[l].partition_broadcast(P)).then_inc(c_loaded[2], 16)
                act.dma_start(b_rt[:, l, GROUPS:], b_fine[l].partition_broadcast(P)).then_inc(c_loaded[2], 16)

            def copy_qkT(l, s):
                act.wait_ge(rot_turned[l], s + 1)
                j, t = divmod(s, T)
                src = psum[4 + s % 2][:, :].rearrange("p (a s) -> p a s", a=4)
                cols = slice(P * t, P * t + P)
                if l == 0 and j == 2:
                    act.copy(qT[:, 4:6, cols], src[:, 0:2, :])
                    act.copy(kT[:, 4:6, cols], src[:, 2:4, :]).then_inc(qkT_ready[l], 1)
                else:
                    dst, a = ((qT, 0), (kT, 0))[j] if l == 0 else ((qT, 0), (qT, 4), (kT, 0), (kT, 4))[j]
                    act.copy(dst[:, a:a + 4, cols], src).then_inc(qkT_ready[l], 1)

            def copy_pT(l, i):
                act.wait_ge(p_turned[l], i + 1)
                if i >= 2:
                    act.wait_ge(pv_done[l], i - 1)
                act.copy(probT[i % 2], psum[2 + i % 2][:, 0:3 * P]).then_inc(pT_ready[l], 1)

            def experts_of(l, r, g, n):
                no = group_no(r, g)
                act.wait_ge(gated_turned[l], no + 1)
                act.copy(gatedT[0:SLOTS * n, :], psum[5][0:SLOTS * n, 0:SEQ]).then_inc(gatedT_ready[l], 1)

                def copy_hidT(k):
                    act.wait_ge(hid_turned[l], expert_no(r, g, k) + 1)
                    act.copy(hidT[k], psum[4][:, 0:P]).then_inc(hidT_ready[l], 1)

                for k in range(n):
                    act.wait_ge(gate_up_done[l], gu_count(r, g, k))
                    if k >= 2:
                        act.wait_ge(hid_ready[l], expert_no(r, g, k) - 1)
                    bank = psum[2 + k % 2]
                    act.activation(eg[k % 2], bank[:, 0:P], ACT.Exp, scale=-1.0)
                    act.copy(gu[k % 2], bank[:, 0:2 * P]).then_inc(gate_up_out[l], 1)
                    if k:
                        copy_hidT(k - 1)
                copy_hidT(n - 1)
                act.wait_ge(down_done[l], no + 1)
                act.copy(y_sb[0:SLOTS * n, 0:512], psum[6][0:SLOTS * n, :]).then_inc(y_low[l], 1)

            for l in range(LAYERS):
                for s in range(NW * T + 2):
                    j, t = divmod(s, T)
                    if n_rot[l] <= s < NW * T:
                        act.wait_ge(proj_done[l], s + 1)
                        if l == 0 and j == NW - 1:
                            act.activation(rg[:, t, :], psum[s % 4][:, :], ACT.Exp, scale=-1.0).then_inc(rg_exp, 1)
                        else:
                            at = 512 * (j - ROTATED[l])
                            act.copy(v_sb[:, t, at:at + 512], psum[s % 4][:, :]).then_inc(bank_out[l][s % 4], 1)
                    if 0 <= s - 2 < n_rot[l]:
                        copy_qkT(l, s - 2)
                for i in range(HEADS[l] + 2):
                    if i < HEADS[l]:
                        act.wait_ge(negm_ready[l], i + 1)
                        b = prob[i % 3]
                        if l == 0:
                            act.activation(b[:, 0:P], b[:, 0:P], ACT.Exp, bias=negm[:, i, 0:1],
                                           accum_out=den[:, 0, i:i + 1])
                            act.activation(b[:, P:3 * P], b[:, P:3 * P], ACT.Exp, bias=negm[:, i, 1:2],
                                           accum_out=den[:, 1, i:i + 1]).then_inc(p_ready[l], 1)
                        else:
                            act.activation(b[:, 0:P], b[:, 0:P], ACT.Exp, bias=negm[:, i, 0:1])
                            act.activation(b[:, P:3 * P], b[:, P:3 * P], ACT.Exp, bias=negm[:, i, 1:2])\
                               .then_inc(exp_done[l], 1)
                    if i >= 2:
                        copy_pT(l, i - 2)
                for n in range(2 * T):
                    act.wait_ge(o_turned[l], n + 1)
                    t, q = divmod(n, 2)
                    act.copy(oT[:, 4 * q:4 * q + 4, P * t:P * t + P],
                             psum[n][:, :].rearrange("p (a s) -> p a s", a=4)).then_inc(oT_ready[l], 1)
                act.wait_ge(gmax_ready[l], 1)
                for t in range(T):
                    act.activation(expg[:, t, :], lg[:, t, 0:GROUPS], ACT.Exp, bias=gv[:, t:t + 1],
                                   accum_out=gv[:, 2 + t:3 + t])
                act.activation(gv[:, 4:6], gv[:, 6:8], ACT.Exp).then_inc(gexp_done[l], 1)
                if l == LAYERS - 1:
                    act.dma_start(gain_row, final_norm.partition_broadcast(P)).then_inc(fin_loaded, 16)
                act.wait_ge(rounds_ready[l], 1)
                more = act.value_load(rounds_i[0:1, l:l + 1], min_val=0, max_val=MAX_ROUNDS - 1)
                with act.Fori(0, more + 1) as r:
                    with act.Fori(0, FULL) as g:
                        experts_of(l, r, g, GE)
                    experts_of(l, r, FULL, TAIL)

        @block.tensor
        def _(pe):
            pe.wait_ge(c_loaded[0], 16)

            def turn_xn(ph):
                for t in range(T):
                    pe.wait_ge(xn_ready, ph * T + t + 1)
                    for q in range(2):
                        for c in range(4):
                            last = pe.transpose(psum[2 * t + q][:, P * c:P * c + P], xn_c[:, t, 4 * q + c, :], ident)
                        last.then_inc(xn_turned, 1)

            def project(l, s):
                j, t = divmod(s, T)
                pe.wait_ge(w_arrived[l][j], 16)
                if s >= 4:
                    pe.wait_ge(bank_out[l][s % 4], s // 4)
                for c in range(C):
                    last = pe.matmul(psum[s % 4][:, :], xnT[:, c, P * t:P * t + P],
                                     ring[:, j, 512 * c:512 * c + 512], start=(c == 0), stop=(c == C - 1))
                last.then_inc(proj_done[l], 1)

            def turn_rot(l, s):
                pe.wait_ge(rot_ready[l], s + 1)
                if s >= 2:
                    pe.wait_ge(qkT_ready[l], s - 1)
                for a in range(4):
                    last = pe.transpose(psum[4 + s % 2][:, P * a:P * a + P], rot[s % 3][:, P * a:P * a + P], ident)
                last.then_inc(rot_turned[l], 1)

            def scores(l, i):
                if 0 <= i - 2 < HEADS[l]:
                    pe.wait_ge(s_out[l], i - 1)
                elif i >= 2:
                    pe.wait_ge(ret_ready, i - 1 - HEADS[l])
                bank = psum[i % 2]
                if i < HEADS[l]:
                    a, lo = i // 2, HEAD * (i % 2)
                    q, k = qT[lo:lo + HEAD, a, :], kT[lo:lo + HEAD, a, :]
                    pe.matmul(bank[:, 0:P], q[:, 0:P], k[:, 0:P], start=True, stop=True)
                    last = pe.matmul(bank[:, P:3 * P], q[:, P:SEQ], k[:, :], start=True, stop=True)
                else:
                    i -= HEADS[l]
                    a, lo = 4 + i // 2, HEAD * (i % 2)
                    q, k = qT[lo:lo + HEAD, a, :], kT[lo:lo + HEAD, a, :]
                    pe.matmul(bank[:, 0:2 * P], k[:, 0:P], q[:, :], start=True, stop=True)
                    last = pe.matmul(bank[:, 2 * P:3 * P], k[:, P:SEQ], q[:, P:SEQ], start=True, stop=True)
                last.then_inc(s_done[l], 1)

            def turn_p(l, i):
                pe.wait_ge(p_ready[l], i + 1)
                if i >= 2:
                    pe.wait_ge(pT_ready[l], i - 1)
                for b in range(3):
                    last = pe.transpose(psum[2 + i % 2][:, P * b:P * b + P], prob[i % 3][:, P * b:P * b + P], ident)
                last.then_inc(p_turned[l], 1)

            def values(l, i):
                if i < HEADS[l]:
                    pe.wait_ge(pT_ready[l], i + 1)
                    w, at, pT = HEAD, HEAD * i, probT[i % 2]
                    banks, col = (psum[4 + 2 * (i // 8)], psum[5 + 2 * (i // 8)]), HEAD * (i % 8)
                    blocks = ((0, 0, 0), (1, 1, 0), (1, 2, 1))
                else:
                    n = i - HEADS[l]
                    pe.wait_ge(ret_ready, n + 1)
                    w, at, pT = P, 512 + P * n, prob[i % 3]
                    banks, col = (psum[6], psum[7]), P * n
                    blocks = ((0, 0, 0), (1, 1, 0), (1, 2, 1))
                for t, b, kt in blocks:
                    last = pe.matmul(banks[t][:, col:col + w], pT[:, P * b:P * b + P], v_sb[:, kt, at:at + w],
                                     start=(kt == 0), stop=(t == kt))
                last.then_inc(pv_done[l], 1)

            def experts_of(l, r, g, n):
                no = group_no(r, g)
                rows = SLOTS * n
                pe.wait_ge(onehot_ready[l], no + 1)
                for t in range(T):
                    last = pe.transpose(psum[5][0:SLOTS * GE, P * t:P * t + P],
                                        gated[:, t, :, :].rearrange("p k s -> p (k s)"), ident)
                last.then_inc(gated_turned[l], 1)
                for c in range(C):
                    for t in range(T):
                        last = pe.matmul(psum[c // 4][:, rows * (c % 4):rows * (c % 4) + rows],
                                         xn_c[:, t, c, :], onehot[:, t, 0:n, :].rearrange("p k s -> p (k s)"),
                                         start=(t == 0), stop=(t == T - 1))
                    if c % 4 == 3:
                        last.then_inc(gathered[l], 1)
                pe.wait_ge(xT_ready[l], no * 2 + 2)

                def turn_hid(k):
                    e = expert_no(r, g, k)
                    pe.wait_ge(hid_ready[l], e + 1)
                    if k:
                        pe.wait_ge(hidT_ready[l], e)
                    pe.transpose(psum[4][:, 0:P], hid[k % 2], ident).then_inc(hid_turned[l], 1)

                for k in range(n):
                    e = expert_no(r, g, k)
                    if k >= 2:
                        pe.wait_ge(gate_up_out[l], e - 1)
                    pe.wait_ge(e_arrived[l][2 * k], arrivals(2 * k, r, g))
                    pe.wait_ge(e_arrived[l][2 * k + 1], arrivals(2 * k + 1, r, g))
                    bank = psum[2 + k % 2]
                    for c in range(C):
                        for j in range(4):
                            last = pe.matmul(
                                bank[32 * j:32 * j + 32, 0:2 * P].rearrange("p (a s) -> p a s", a=2),
                                xT[:, c, SLOTS * k:SLOTS * k + SLOTS],
                                ring[:, 2 * k:2 * k + 2, 512 * c + P * j:512 * c + P * j + P],
                                start=(c == 0), stop=(c == C - 1), tile_position=(0, 32 * j))
                    last.then_inc(gate_up_done[l], 1 if n == GE or k < n - 1 else 1 + GE - n)
                    if k:
                        turn_hid(k - 1)
                turn_hid(n - 1)
                for k in range(n):
                    pe.wait_ge(e_arrived[l][6 + k], arrivals(6 + k, r, g))
                pe.wait_ge(hidT_ready[l], expert_no(r, g, n))
                for j in range(HID // P):
                    for half in range(2):
                        for k in range(n):
                            last = pe.matmul(
                                psum[6 + half][32 * k:32 * k + 32, :], hidT[k][:, 32 * j:32 * j + 32],
                                ring[:, 6 + k, D * j + 512 * half:D * j + 512 * half + 512],
                                start=(j == 0), stop=(j == HID // P - 1), tile_position=(0, 32 * k))
                last.then_inc(down_done[l], 1)
                pe.wait_ge(y_low[l], no + 1)
                pe.wait_ge(y_high[l], no + 1)
                pe.wait_ge(gatedT_ready[l], no + 1)
                for q in range(4):
                    t, half = divmod(q, 2)
                    if q >= 2:
                        pe.wait_ge(added[l], no * 4 + (q - 1))
                    pe.matmul(psum[q % 2][:, :], gatedT[0:rows, P * t:P * t + P],
                              y_sb[0:rows, 512 * half:512 * half + 512], start=True, stop=True)\
                      .then_inc(scattered[l], 1)

            for l in range(LAYERS):
                turn_xn(2 * l)
                pe.wait_ge(xnT_ready, 4 * (2 * l) + 4)
                for s in range(NW * T + 2):
                    if s < NW * T:
                        project(l, s)
                    if 0 <= s - 2 < n_rot[l]:
                        turn_rot(l, s - 2)
                pe.wait_ge(qkT_ready[l], n_rot[l])
                for b in range(4):
                    pe.wait_ge(bank_out[l][b], 3)
                for i in range(n_items[l] + 3):
                    if i < n_items[l]:
                        scores(l, i)
                    if 0 <= i - 2 < HEADS[l]:
                        turn_p(l, i - 2)
                    if 0 <= i - 3:
                        values(l, i - 3)
                for n in range(2 * T):
                    t, q = divmod(n, 2)
                    pe.wait_ge(o_ready[l], T * 2 if l == 0 else T * 2)
                    for c in range(4):
                        last = pe.transpose(psum[n][:, P * c:P * c + P],
                                            o_sb[:, t, P * (4 * q + c):P * (4 * q + c) + P], ident)
                    last.then_inc(o_turned[l], 1)
                pe.wait_ge(oT_ready[l], 4)
                for n in range(2):
                    pe.wait_ge(w_arrived[l][6 + n], 16)
                    for t in range(T):
                        for c in range(C):
                            last = pe.matmul(psum[4 + 2 * n + t][:, :], oT[:, c, P * t:P * t + P],
                                             ring[:, 6 + n, 512 * c:512 * c + 512], start=(c == 0), stop=(c == C - 1))
                        last.then_inc(mixed[l], 1)
                pe.wait_ge(mix_added[l], 4)
                turn_xn(2 * l + 1)
                pe.wait_ge(xnT_ready, 4 * (2 * l + 1) + 4)
                pe.wait_ge(c_loaded[2], 12 * 16)
                for t in range(T):
                    for c in range(C):
                        last = pe.matmul(psum[4][:, 64 * t:64 * t + 36], xnT[:, c, P * t:P * t + P],
                                         w_rt[:, l, c, :], start=(c == 0), stop=(c == C - 1))
                last.then_inc(logits_done[l], 1)
                pe.wait_ge(assigned[l], 1)
                before, ones = const("before"), const("ones")
                pe.matmul(psum[5][:, 0:32], before, asg[:, 0, :], start=True, stop=True)
                pe.matmul(psum[5][:, 32:64], ones, asg[:, 0, :], start=True, stop=False)
                pe.matmul(psum[5][:, 32:64], before, asg[:, 1, :], start=False, stop=True)
                pe.matmul(psum[5][:, 64:96], ones, asg[:, 0, :], start=True, stop=False)
                pe.matmul(psum[5][:, 64:96], ones, asg[:, 1, :], start=False, stop=True).then_inc(pos_done[l], 1)
                pe.wait_ge(rounds_ready[l], 1)
                more = pe.value_load(rounds_i[0:1, l:l + 1], min_val=0, max_val=MAX_ROUNDS - 1)
                with pe.Fori(0, more + 1) as r:
                    with pe.Fori(0, FULL) as g:
                        experts_of(l, r, g, GE)
                    experts_of(l, r, FULL, TAIL)

        @block.vector
        def _(dve):
            norm_chain = Chain(dve, dve_norm)
            dve.wait_ge(c_loaded[1], 16)
            dve.wait_ge(c_loaded[0], 16)
            dve.wait_ge(c_loaded[2], 12 * 16)

            def normalise(ph):
                link = norm_chain.link
                for t in range(T):
                    last = dve.tensor_tensor_reduce(xn_t[:, t, :], h[:, t, :], h[:, t, :], 1.0, 0.0,
                                                    ALU.mult, ALU.add, sumsq[:, t:t + 1])
                link(last)
                dve.tensor_scalar(var, sumsq, 1.0 / D, EPS, ALU.mult, ALU.add).then_inc(var_ready, 1)
                dve.wait_ge(pow_ready, ph + 2)
                link(dve.tensor_tensor(newt, rstd, rstd, ALU.mult))
                link(dve.tensor_tensor(newt, newt, var, ALU.mult))
                link(dve.tensor_scalar(newt, newt, -0.5, 1.5, ALU.mult, ALU.add))
                link(dve.tensor_tensor(rstd, rstd, newt, ALU.mult))
                if ph == 2 * LAYERS:
                    dve.wait_ge(fin_loaded, 16)
                for t in range(T):
                    if ph < 2 * LAYERS:
                        dve.tensor_scalar(xn_c[:, t, :, :], h[:, t, :].rearrange("p (q c) -> p c q", c=C),
                                          rstd[:, t:t + 1], None, ALU.mult).then_inc(xn_ready, 1)
                    else:
                        dve.scalar_tensor_tensor(out=xn_t[:, t, :], in0=h[:, t, :], scalar=rstd[:, t:t + 1],
                                                 in1=gain_row, op0=ALU.mult, op1=ALU.mult).then_inc(xn_ready, 1)
                if ph == 2 * LAYERS:
                    return
                for n in range(2 * T):
                    t, q = divmod(n, 2)
                    dve.wait_ge(xn_turned, 4 * ph + n + 1)
                    dve.tensor_tensor(xnT[:, 4 * q:4 * q + 4, P * t:P * t + P],
                                      psum[n][:, :].rearrange("p (a s) -> p a s", a=4),
                                      gains[:, ph, 4 * q:4 * q + 4].unsqueeze(2).broadcast_to([P, 4, P]),
                                      ALU.mult).then_inc(xnT_ready, 1)

            def rotate(l, s, link):
                j, t = divmod(s, T)
                dve.wait_ge(proj_done[l], s + 1)
                if s >= 3:
                    dve.wait_ge(rot_turned[l], s - 2)
                kind = "ret" if l == 0 and j == 2 else "rope"
                form = "p (h d x) -> p h d x" if kind == "ret" else "p (h x d) -> p h x d"

                def halves(ap, n):
                    v = ap.rearrange(form, h=n, x=2)
                    return (v[:, :, :, 0], v[:, :, :, 1]) if kind == "ret" else (v[:, :, 0, :], v[:, :, 1, :])

                cos = const(kind + "_cos", T, HEAD)[:, t, :]
                sin = const(kind + "_sin", T, HEAD)[:, t, :]
                bank = psum[s % 4][:, :]
                dve.tensor_tensor(rot[s % 3].rearrange("p (h d) -> p h d", h=8),
                                  bank.rearrange("p (h d) -> p h d", h=8),
                                  cos.unsqueeze(1).broadcast_to([P, 8, HEAD]), ALU.mult)
                src, dst, sn = halves(bank, 8), halves(rot_tmp, 8), halves(sin, 1)
                for a in range(2):
                    last = dve.tensor_tensor(dst[a], src[1 - a], sn[a].broadcast_to([P, 8, HEAD // 2]), ALU.mult)
                last.then_inc(bank_out[l][s % 4], 1)
                dve.wait_ge(bank_out[l][s % 4], s // 4 + 1)
                dve.tensor_tensor(rot[s % 3], rot[s % 3], rot_tmp, ALU.add).then_inc(rot_ready[l], 1)
                dve.wait_ge(rot_ready[l], s + 1)

            def head_max(l, i, link):
                dve.wait_ge(s_done[l], i + 1)
                if i >= 3:
                    dve.wait_ge(p_turned[l], i - 2)
                mask = const("mask0" if l == 0 else "mask1")
                for t, cols in ((0, slice(0, P)), (1, slice(P, 3 * P))):
                    last = dve.tensor_tensor_reduce(prob[i % 3][:, cols], psum[i % 2][:, cols], mask[:, cols],
                                                    HEAD ** -0.5, -FAR, ALU.add, ALU.max, mx[:, i, t:t + 1])
                last.then_inc(s_out[l], 1)
                dve.wait_ge(s_out[l], i + 1)
                dve.tensor_scalar(negm[:, i, :], mx[:, i, :], -1.0, None, ALU.mult).then_inc(negm_ready[l], 1)

            def head_count(i):
                dve.wait_ge(exp_done[1], i + 1)
                count = const("count1")
                for t, cols in ((0, slice(0, P)), (1, slice(P, 3 * P))):
                    last = dve.tensor_tensor_reduce(prob[i % 3][:, cols], prob[i % 3][:, cols], count[:, cols],
                                                    1.0, 0.0, ALU.mult, ALU.add, den[:, t, i:i + 1])
                last.then_inc(p_ready[1], 1)

            def head_norm(l, q, link):
                dve.wait_ge(pv_done[l], 8 * q + 8)
                dve.wait_ge(p_ready[l], 8 * q + 8)
                link(dve.reciprocal(rden[:, :, 8 * q:8 * q + 8], den[:, :, 8 * q:8 * q + 8]))
                for t in range(T):
                    dve.tensor_tensor(o_sb[:, t, 512 * q:512 * q + 512].rearrange("p (h d) -> p h d", h=8),
                                      psum[4 + 2 * q + t][:, :].rearrange("p (h d) -> p h d", h=8),
                                      rden[:, t, 8 * q:8 * q + 8].unsqueeze(2).broadcast_to([P, 8, HEAD]),
                                      ALU.mult).then_inc(o_ready[l], 1)

            def route(l, link):
                dve.wait_ge(logits_done[l], 1)
                for t in range(T):
                    link(dve.memset(lg[:, t, :], -FAR))
                lgt = psum[4][:, 0:128].rearrange("p (t e) -> p t e", t=T)
                bias = b_rt[:, l, :].unsqueeze(1).broadcast_to([P, T, GROUPS + EXPERTS])
                dve.tensor_tensor(lg[:, :, 0:GROUPS], lgt[:, :, 0:GROUPS], bias[:, :, 0:GROUPS], ALU.add)
                link(dve.tensor_tensor(lf, lgt[:, :, GROUPS:36], bias[:, :, GROUPS:36], ALU.add))
                for t in range(T):
                    link(dve.max(top[:, t, :], lg[:, t, :]))
                for t in range(T):
                    last = dve.max_index(idx_u[:, t, :], top[:, t, :], lg[:, t, :])
                link(last)
                link(dve.tensor_copy(idx[:, 0:2], idx_u[:, 0:2, 0]))
                dve.tensor_scalar(gv[:, 0:2], top[:, 0:2, 0], -1.0, None, ALU.mult)
                for t in range(T):
                    last = dve.tensor_scalar(gmask[:, t, :], const("iota")[:, 0:GROUPS], idx[:, t:t + 1], None,
                                             ALU.is_equal)
                link(last)
                link(dve.tensor_scalar(pen, gmask, FAR, -FAR, ALU.mult, ALU.add))
                by_group = "p (g e) -> p g e"
                for t in range(T):
                    m, f = masked[:, t, :].rearrange(by_group, g=GROUPS), lf[:, t, :].rearrange(by_group, g=GROUPS)
                    link(dve.tensor_tensor(m, f, gmask[:, t, :].unsqueeze(2).broadcast_to([P, GROUPS, 8]), ALU.mult))
                    link(dve.tensor_tensor(m, m, pen[:, t, :].unsqueeze(2).broadcast_to([P, GROUPS, 8]), ALU.add))
                for t in range(T):
                    link(dve.max(top[:, T + t, :], masked[:, t, :]))
                for t in range(T):
                    last = dve.max_index(idx_u[:, T + t, :], top[:, T + t, :], masked[:, t, :])
                link(last)
                dve.tensor_copy(idx[:, 2:4], idx_u[:, 2:4, 0])
                link(dve.tensor_copy(idx[:, 4:6], idx_u[:, 2:4, 1]))
                dve.tensor_tensor(gv[:, 6:8], top[:, 2:4, 1], top[:, 2:4, 0], ALU.subtract).then_inc(gmax_ready[l], 1)
                for t in range(T):
                    dve.tensor_scalar(first[:, t, :], const("iota"), idx[:, 2 + t:3 + t], None, ALU.is_equal)
                    last = dve.tensor_scalar(second[:, t, :], const("iota"), idx[:, 4 + t:5 + t], None, ALU.is_equal)
                link(last)
                dve.tensor_tensor(asg[:], first, second, ALU.add).then_inc(assigned[l], 1)
                dve.wait_ge(gexp_done[l], 1)
                link(dve.tensor_scalar(gv[:, 8:10], gv[:, 4:6], 1.0, None, ALU.add))
                link(dve.tensor_tensor(gv[:, 8:10], gv[:, 8:10], gv[:, 2:4], ALU.mult))
                link(dve.reciprocal(gv[:, 10:12], gv[:, 8:10]))
                link(dve.tensor_tensor(gv[:, 12:14], gv[:, 10:12], gv[:, 4:6], ALU.mult))
                for t in range(T):
                    link(dve.tensor_scalar(gate[:, t, 0:EXPERTS], first[:, t, :], gv[:, 10 + t:11 + t], None, ALU.mult))
                    link(dve.scalar_tensor_tensor(out=gate[:, t, 0:EXPERTS], in0=second[:, t, :],
                                                  scalar=gv[:, 12 + t:13 + t], in1=gate[:, t, 0:EXPERTS],
                                                  op0=ALU.mult, op1=ALU.add))
                dve.wait_ge(pos_done[l], 1)
                pos = psum[5][:, 0:64].rearrange("p (t e) -> p t e", t=T)
                link(dve.scalar_tensor_tensor(out=posm[:, :, 0:EXPERTS], in0=pos, scalar=1.0, in1=asg[:],
                                              op0=ALU.add, op1=ALU.mult))
                link(dve.tensor_scalar(posm[:, :, 0:EXPERTS], posm[:, :, 0:EXPERTS], -1.0, None, ALU.add))
                link(dve.reduce_max(cnt[:, 0:1], psum[5][:, 64:96], AX.X))
                link(dve.tensor_scalar(limhit[:], const("limits"), cnt[:, 0:1], None, ALU.is_lt))
                link(dve.reduce_sum(rounds_f[:, 0:1], limhit[:], AX.X))
                dve.tensor_scalar(rounds_i[:, l:l + 1], rounds_f[:, 0:1], -1.0, None, ALU.add)\
                   .then_inc(rounds_ready[l], 1)

            def experts_of(l, r, g, n, first_expert, base):
                chain = Chain(dve, dve_moe[l], base)
                no = group_no(r, g)
                cols = bass.ds(first_expert, n)
                chain.link(dve.tensor_tensor(
                    onehot[:, :, 0:n, :], const("iota").unsqueeze(1).unsqueeze(1).broadcast_to([P, T, n, SLOTS]),
                    posm[:, :, cols].unsqueeze(3).broadcast_to([P, T, n, SLOTS]), ALU.is_equal))
                dve.tensor_tensor(gated[:, :, 0:n, :], onehot[:, :, 0:n, :],
                                  gate[:, :, cols].unsqueeze(3).broadcast_to([P, T, n, SLOTS]), ALU.mult)\
                   .then_inc(onehot_ready[l], 1)
                for q in range(2):
                    dve.wait_ge(gathered[l], no * 2 + (q + 1))
                    dve.tensor_tensor(xT[:, 4 * q:4 * q + 4, 0:SLOTS * n],
                                      psum[q][:, 0:4 * SLOTS * n].rearrange("p (a s) -> p a s", a=4),
                                      gains[:, 2 * l + 1, 4 * q:4 * q + 4].unsqueeze(2).broadcast_to([P, 4, SLOTS * n]),
                                      ALU.mult).then_inc(xT_ready[l], 1)
                for k in range(n):
                    e = expert_no(r, g, k)
                    dve.wait_ge(gate_up_out[l], e + 1)
                    if k >= 2:
                        dve.wait_ge(hid_turned[l], e - 1)
                    eb, gb = eg[k % 2], gu[k % 2]
                    chain.link(dve.tensor_scalar(eb, eb, 1.0, None, ALU.add))
                    chain.link(dve.reciprocal(eb, eb))
                    chain.link(dve.tensor_tensor(eb, eb, gb[:, 0:P], ALU.mult))
                    dve.tensor_tensor(hid[k % 2], eb, gb[:, P:2 * P], ALU.mult).then_inc(hid_ready[l], 1)
                dve.wait_ge(down_done[l], no + 1)
                dve.tensor_copy(y_sb[0:SLOTS * n, 512:1024], psum[7][0:SLOTS * n, :]).then_inc(y_high[l], 1)
                for q in range(4):
                    t, half = divmod(q, 2)
                    dve.wait_ge(scattered[l], no * 4 + (q + 1))
                    hv = h[:, t, 512 * half:512 * half + 512]
                    dve.tensor_tensor(hv, hv, psum[q % 2][:, :], ALU.add).then_inc(added[l], 1)
                return chain.n

            for l in range(LAYERS):
                normalise(2 * l)
                attn_chain = Chain(dve, dve_attn[l])
                link = attn_chain.link
                for s in range(n_rot[l]):
                    rotate(l, s, link)
                if l == 0:
                    for t in range(T):
                        s = (NW - 1) * T + t
                        dve.wait_ge(rg_exp, t + 1)
                        link(dve.tensor_scalar(rg[:, t, :], rg[:, t, :], 1.0, None, ALU.add))
                        link(dve.reciprocal(rg[:, t, :], rg[:, t, :]))
                        dve.tensor_tensor(rg[:, t, :], rg[:, t, :], psum[s % 4][:, :], ALU.mult)\
                           .then_inc(bank_out[l][s % 4], 1)
                for i in range(n_items[l] + 4):
                    if i < HEADS[l]:
                        head_max(l, i, link)
                    elif i < n_items[l]:
                        n = i - HEADS[l]
                        dve.wait_ge(s_done[l], i + 1)
                        if n < 3:
                            dve.wait_ge(p_turned[l], i - 2)
                        else:
                            dve.wait_ge(pv_done[l], i - 2)
                        dk = const("decay", RET, 2 * P)[:, n, :]
                        dve.tensor_tensor(prob[i % 3][:, 0:2 * P], psum[i % 2][:, 0:2 * P], dk, ALU.mult)
                        dve.tensor_tensor(prob[i % 3][:, 2 * P:3 * P], psum[i % 2][:, 2 * P:3 * P], dk[:, 0:P],
                                          ALU.mult).then_inc(ret_ready, 1)
                        dve.wait_ge(ret_ready, n + 1)
                    if l == 1 and 1 <= i <= HEADS[l]:
                        head_count(i - 1)
                    if i == 11:
                        head_norm(l, 0, link)
                if l == 1:
                    head_norm(l, 1, link)
                else:
                    dve.wait_ge(pv_done[l], n_items[l])
                    for t in range(T):
                        for n in range(RET):
                            last = dve.bn_stats(bnst[:, RET * t + n, :], psum[6 + t][:, P * n:P * n + P])
                    link(last)
                    for t in range(T):
                        for n in range(RET):
                            last = dve.bn_aggr(rstat[:, t, n, :], bnst[:, RET * t + n, :])
                    link(last)
                    dve.tensor_scalar(rvar.rearrange("p (t h) -> p t h", t=T), rstat[:, :, :, 1], EPS, None, ALU.add)\
                       .then_inc(ret_var, 1)
                    dve.wait_ge(ret_var, 1)
                    dve.wait_ge(ret_pow, 1)
                    nw8 = small[:, 258:266]
                    link(dve.tensor_tensor(nw8, rrstd, rrstd, ALU.mult))
                    link(dve.tensor_tensor(nw8, nw8, rvar, ALU.mult))
                    link(dve.tensor_scalar(nw8, nw8, -0.5, 1.5, ALU.mult, ALU.add))
                    link(dve.tensor_tensor(rrstd, rrstd, nw8, ALU.mult))
                    for t in range(T):
                        for n in range(RET):
                            m = RET * t + n
                            last = dve.tensor_scalar(o_sb[:, t, 512 + P * n:512 + P * n + P], psum[6 + t][:, P * n:P * n + P],
                                                     rstat[:, t, n, 0:1], rrstd[:, m:m + 1], ALU.subtract, ALU.mult)
                        link(last)
                        dve.tensor_tensor(o_sb[:, t, 512:1024], o_sb[:, t, 512:1024], rg[:, t, :], ALU.mult)\
                           .then_inc(o_ready[l], 1)
                for n in range(2):
                    for t in range(T):
                        dve.wait_ge(mixed[l], 2 * n + t + 1)
                        hv = h[:, t, 512 * n:512 * n + 512]
                        dve.tensor_tensor(hv, hv, psum[4 + 2 * n + t][:, :], ALU.add).then_inc(mix_added[l], 1)
                dve.wait_ge(mix_added[l], 4)
                normalise(2 * l + 1)
                route_chain = Chain(dve, dve_route[l])
                route(l, route_chain.link)
                dve.wait_ge(rounds_ready[l], 1)
                more = dve.value_load(rounds_i[0:1, l:l + 1], min_val=0, max_val=MAX_ROUNDS - 1)
                with dve.Fori(0, more + 1) as r:
                    with dve.Fori(0, FULL) as g:
                        n = experts_of(l, r, g, GE, g * GE, r * DVE_ROUND + g * DVE_GROUP)
                        assert n == DVE_GROUP
                    base = r * DVE_ROUND + FULL * DVE_GROUP
                    n = experts_of(l, r, FULL, TAIL, FULL * GE, base)
                    chain = Chain(dve, dve_moe[l], base + n)
                    chain.link(dve.tensor_scalar(posm[:, :, 0:EXPERTS], posm[:, :, 0:EXPERTS], -float(SLOTS), None,
                                                 ALU.add))
                    assert FULL * DVE_GROUP + n + 1 == DVE_ROUND
                dve.wait_ge(added[l], group_no(more, FULL) * 4 + 4)
            normalise(2 * LAYERS)


_INS = ['x', 'mix_norm_even', 'w_in_even', 'w_out_even', 'mix_norm_odd', 'w_in_odd', 'w_out_odd', 'ffn_norm',
        'w_router_group', 'b_router_group', 'w_router_expert', 'b_router_expert', 'w_expert_gate',
        'w_expert_up', 'w_expert_down', 'final_norm']


def kernel(**inputs):
    import concourse.bacc as _bacc
    from concourse.bass_utils import run_bass_kernel_spmd as _run

    nc = _bacc.Bacc("TRN2", target_bir_lowering=False, num_devices=1)
    arrays, args = {}, []
    for name in _INS:
        a = np.ascontiguousarray(inputs[name])
        arrays[f"in_{name}"] = a
        args.append(nc.dram_tensor(f"in_{name}", a.shape, mybir.dt.from_np(a.dtype), kind="ExternalInput").ap())
    arrays["shape_consts"] = shape_constants()
    args.append(nc.dram_tensor("shape_consts", (P, CONST_COLS), F32, kind="ExternalInput").ap())
    args.append(nc.dram_tensor("out_0", (1, SEQ, D), F32, kind="ExternalOutput").ap())
    build(nc, *args)
    r = _run(nc, [arrays], core_ids=[0])
    return r.results[0]["out_0"]
```

```python
from contextlib import ExitStack

import numpy as np

import concourse.bass as bass
from concourse import mybir

F32 = mybir.dt.float32
I32 = mybir.dt.int32
U32 = mybir.dt.uint32
ALU = mybir.AluOpType
ACT = mybir.ActivationFunctionType
AX = mybir.AxisListType

P = 128
D = 1024
SEQ = 256
T = SEQ // P
C = D // P
LAYERS = 2
HEAD = 64
NW = 6
HEADS = (8, 16)
RET = 4
ROTATED = (3, 4)
BLOCKS = ((0, 1, 3, 2, 4, 5), (0, 1, 2, 3, 4, 5))
EXPERTS = 32
GROUPS = 4
SLOTS = 32
GE = 3
FULL = EXPERTS // GE
TAIL = EXPERTS - FULL * GE
HID = 512
MAX_ROUNDS = SEQ // SLOTS
EPS = 1e-6
FAR = 3.0e38
UNIT = 4096

CONST_WIDTHS = (
    ("ident", P),
    ("rope_cos", T * HEAD), ("rope_sin", T * HEAD), ("ret_cos", T * HEAD), ("ret_sin", T * HEAD),
    ("mask0", 3 * P), ("decay", RET * 2 * P), ("before", P), ("ones", P), ("iota", 32), ("limits", 8),
    ("mask1", 3 * P), ("count1", 3 * P),
)
FIRST_CONSTS = P + 4 * T * HEAD
CONST_AT = {}
_at = 0
for _name, _w in CONST_WIDTHS:
    CONST_AT[_name] = (_at, _w)
    _at += _w
CONST_COLS = _at


def shape_constants():
    f = np.float32
    out = np.zeros((P, CONST_COLS), f)

    def put(name, a):
        at, w = CONST_AT[name]
        out[:, at:at + w] = np.asarray(a, f).reshape(P, w)

    i = np.arange(P)
    put("ident", np.eye(P))
    put("before", i[:, None] < i[None, :])
    put("ones", np.ones((P, P)))
    put("iota", np.tile(np.arange(32), (P, 1)))
    put("limits", np.tile(np.arange(8) * SLOTS, (P, 1)))
    q, k = i[:, None], i[None, :]
    causal = np.where(k <= q, 0.0, -1e30)
    put("mask0", np.concatenate([causal, np.zeros((P, P)), causal], 1))

    def windows(dist):
        n = np.zeros(dist.shape)
        for window, dil in ((128, 1), (512, 4), (2048, 16)):
            n += (dist >= 0) & (dist % dil == 0) & (dist // dil <= window // dil)
        return n

    near, far = windows(q - k), windows(q + P - k)
    count = np.concatenate([near, far, near], 1)
    put("count1", count)
    put("mask1", np.where(count > 0, 0.0, -1e30))
    half = HEAD // 2
    pos = np.arange(SEQ, dtype=f)[:, None]
    inv = (f(1.0) / (f(10000.0) ** (np.arange(half, dtype=f) * f(2.0 / HEAD)))).astype(f)
    ang = pos * inv[None, :]
    cos, sin = np.cos(ang).astype(f), np.sin(ang).astype(f)
    tok = lambda a: a.reshape(T, P, -1).transpose(1, 0, 2)
    put("rope_cos", tok(np.concatenate([cos, cos], 1)))
    put("rope_sin", tok(np.concatenate([-sin, sin], 1)))
    freq = (f(1.0) / (f(10000.0) ** np.linspace(0.0, 1.0, half, dtype=f))).astype(f)
    ang = pos * freq[None, :]
    cos, sin = np.cos(ang).astype(f), np.sin(ang).astype(f)
    put("ret_cos", tok(np.stack([cos, cos], -1).reshape(SEQ, HEAD)))
    put("ret_sin", tok(np.stack([-sin, sin], -1).reshape(SEQ, HEAD)))
    rel = np.arange(SEQ)[None, :] - i[:, None]
    decay = []
    for h in range(RET):
        log_gamma = np.log(1.0 - 2.0 ** (-5.0 - h))
        decay.append(np.where(rel >= 0, np.exp(log_gamma * np.maximum(rel, 0)), 0.0) * HEAD ** -0.5)
    put("decay", np.stack(decay, 1))
    return out


class Chain:

    def __init__(self, eng, sem, base=0):
        self.eng, self.sem, self.base, self.n = eng, sem, base, 0

    def link(self, ins):
        self.n += 1
        ins.then_inc(self.sem, 1)
        self.eng.wait_ge(self.sem, self.base + self.n)


def group_no(r, g):
    return r * (FULL + 1) + g


def expert_no(r, g, k):
    return r * EXPERTS + g * GE + k


def gu_count(r, g, k):
    return r * ((FULL + 1) * GE) + g * GE + (k + 1)


def arrivals(pos, r, g):
    per_round = FULL if pos in (4, 5, 8) else FULL + 1
    return (r * per_round + g + 1) * 16


DVE_GROUP = 1 + 3 * GE
DVE_ROUND = FULL * DVE_GROUP + 1 + 3 * TAIL + 1


def build(nc, x, mix_even, w_in_even, w_out_even, mix_odd, w_in_odd, w_out_odd, ffn_norm,
          w_group, b_group, w_fine, b_fine, w_gate, w_up, w_down, final_norm, consts, out):
    w_in = (w_in_even, w_in_odd)
    w_out = (w_out_even, w_out_odd)
    mix = (mix_even, mix_odd)
    with ExitStack() as ctx:
        def sb(name, shape, dt=F32):
            return ctx.enter_context(nc.sbuf_tensor(name, shape, dt))

        def sem(name):
            return ctx.enter_context(nc.semaphore(name))

        def sems(name, n):
            return [sem(f"{name}{i}") for i in range(n)]

        ring = sb("ring", [P, 9, UNIT])
        h = sb("h", [P, T, D])
        xn = sb("xn", [P, T * D])
        xnT = sb("xnT", [P, C, SEQ])
        work = sb("work", [P, 5632])
        cst = sb("cst", [P, CONST_COLS])
        gains = sb("gains", [P, 2 * LAYERS, C])
        w_rt = sb("w_rt", [P, LAYERS, C, GROUPS + EXPERTS])
        b_rt = sb("b_rt", [P, LAYERS, GROUPS + EXPERTS])
        small = sb("small", [P, 320])
        idx_u = sb("idx_u", [P, 2 * T, 8], U32)
        rounds_i = sb("rounds_i", [P, LAYERS], I32)
        psum = [ctx.enter_context(nc.psum_tensor(f"bank{i}", [P, 512], F32)) for i in range(8)]

        def const(name, *shape):
            at, w = CONST_AT[name]
            v = cst[:, at:at + w]
            if len(shape) == 2:
                v = v.rearrange("p (a b) -> p a b", a=shape[0])
            return v

        ident = const("ident")
        xn_t = xn[:, :].rearrange("p (t d) -> p t d", t=T)
        xn_c = xn[:, :].rearrange("p (t c q) -> p t c q", t=T, c=C)
        rot = [xn[:, 512 * i:512 * i + 512] for i in range(3)]
        rot_tmp = xn[:, 1536:2048]
        oT = xnT
        qT = ring[:, 8, 0:2048].rearrange("p (a s) -> p a s", a=8)
        kT = ring[:, 7, :].rearrange("p (h s) -> p h s", h=16)
        probT = [xn[:, 384 * i:384 * i + 384] for i in range(4)]
        v_sb = work[:, 0:2048].rearrange("p (t d) -> p t d", t=T)
        rg = work[:, 2048:3072].rearrange("p (t d) -> p t d", t=T)
        prob = [work[:, 3072 + 384 * i:3072 + 384 * i + 384] for i in range(4)]
        o_ret = work[:, 4608:5632].rearrange("p (t d) -> p t d", t=T)
        onehot = work[:, 0:192].rearrange("p (t k s) -> p t k s", t=T, k=GE)
        gated = work[:, 192:384].rearrange("p (t k s) -> p t k s", t=T, k=GE)
        gatedT = work[:, 384:640]
        xT = work[:, 640:1408].rearrange("p (c s) -> p c s", c=C)
        eg = [work[:, 1408 + 128 * i:1536 + 128 * i] for i in range(2)]
        gu = [work[:, 1664 + 256 * i:1920 + 256 * i] for i in range(2)]
        hid = [work[:, 2176 + 128 * i:2304 + 128 * i] for i in range(2)]
        hidT = [work[:, 2432 + 128 * i:2560 + 128 * i] for i in range(GE)]
        y_sb = work[:, 2816:3840]
        masked = work[:, 3840:3904].rearrange("p (t e) -> p t e", t=T)
        first = work[:, 3904:3968].rearrange("p (t e) -> p t e", t=T)
        second = work[:, 3968:4032].rearrange("p (t e) -> p t e", t=T)
        lf = work[:, 4032:4096].rearrange("p (t e) -> p t e", t=T)
        gain_row = work[:, 4096:5120]
        sumsq, var, rstd, newt = (small[:, 2 * i:2 * i + 2] for i in range(4))
        den = small[:, 8:40].rearrange("p (h t) -> p h t", t=T)
        rden = small[:, 40:88].rearrange("p (h b) -> p h b", b=3)
        negm = small[:, 104:136].rearrange("p (h t) -> p h t", t=T)
        sq = small[:, 88:92].rearrange("p (t a) -> p t a", t=T)
        lg = small[:, 136:152].rearrange("p (t e) -> p t e", t=T)
        top = small[:, 152:184].rearrange("p (a e) -> p a e", a=2 * T)
        idx = small[:, 184:192]
        gv = small[:, 192:208]
        pen = small[:, 208:216].rearrange("p (t e) -> p t e", t=T)
        gmask = small[:, 216:224].rearrange("p (t e) -> p t e", t=T)
        rstat = small[:, 224:240].rearrange("p (t h m) -> p t h m", t=T, h=RET)
        rvar = small[:, 240:248]
        rrstd = small[:, 248:256]
        rounds_f = small[:, 256:258]
        bnst = small[:, 258:306].rearrange("p (a s) -> p a s", a=2 * RET)
        expg = small[:, 306:314].rearrange("p (t e) -> p t e", t=T)
        half_exp = small[:, 314:316]
        cnt = small[:, 316:318]
        posm = sb("posm", [P, T, 36])
        gate = sb("gate", [P, T, 36])
        asg = sb("asg", [P, T, EXPERTS])
        limhit = sb("limhit", [P, MAX_ROUNDS])

        x_loaded = sems("x_loaded", T)
        const_loaded = sems("const_loaded", 2)
        gain_loaded = sem("gain_loaded")
        router_loaded = sem("router_loaded")
        w_arrived = [sems(f"w_arrived{l}_", 8) for l in range(LAYERS)]
        e_arrived = [sems(f"e_arrived{l}_", 9) for l in range(LAYERS)]
        fin_loaded = sem("fin_loaded")
        out_stored = sem("out_stored")
        squared = sem("squared")
        var_ready = sem("var_ready")
        pow_ready = sem("pow_ready")
        xn_ready = sem("xn_ready")
        xn_turned = sem("xn_turned")
        xnT_ready = sem("xnT_ready")
        dve_norm = sem("dve_norm")
        proj_done = sems("proj_done", LAYERS)
        bank_out = [sems(f"bank_out{l}_", 4) for l in range(LAYERS)]
        rot_ready = sems("rot_ready", LAYERS)
        rot_turned = sems("rot_turned", LAYERS)
        qkT_ready = sems("qkT_ready", LAYERS)
        rg_exp = sem("rg_exp")
        k_cleared = sems("k_cleared", LAYERS)
        s_done = sems("s_done", LAYERS)
        s_out = sems("s_out", LAYERS)
        exp_done = sems("exp_done", LAYERS)
        den_ready = sems("den_ready", LAYERS)
        p_ready = sems("p_ready", LAYERS)
        p_turned = sems("p_turned", LAYERS)
        pT_ready = sems("pT_ready", LAYERS)
        pair_done = sems("pair_done", LAYERS)
        oT_ready = sems("oT_ready", LAYERS)
        ret_ready = sem("ret_ready")
        ret_done = sem("ret_done")
        ret_var = sem("ret_var")
        ret_pow = sem("ret_pow")
        ret_normed = sem("ret_normed")
        ret_turned = sem("ret_turned")
        retT_ready = sem("retT_ready")
        mixed = sems("mixed", LAYERS)
        mix_added = sems("mix_added", LAYERS)
        dve_attn = sems("dve_attn", LAYERS)
        logits_done = sems("logits_done", LAYERS)
        gmax_ready = sems("gmax_ready", LAYERS)
        gexp_done = sems("gexp_done", LAYERS)
        assigned = sems("assigned", LAYERS)
        pos_done = sems("pos_done", LAYERS)
        rounds_ready = sems("rounds_ready", LAYERS)
        dve_route = sems("dve_route", LAYERS)
        onehot_ready = sems("onehot_ready", LAYERS)
        gated_turned = sems("gated_turned", LAYERS)
        gatedT_ready = sems("gatedT_ready", LAYERS)
        gathered = sems("gathered", LAYERS)
        xT_ready = sems("xT_ready", LAYERS)
        gate_up_done = sems("gate_up_done", LAYERS)
        gate_up_out = sems("gate_up_out", LAYERS)
        hid_ready = sems("hid_ready", LAYERS)
        hid_turned = sems("hid_turned", LAYERS)
        hidT_ready = sems("hidT_ready", LAYERS)
        down_done = sems("down_done", LAYERS)
        y_low = sems("y_low", LAYERS)
        y_high = sems("y_high", LAYERS)
        scattered = sems("scattered", LAYERS)
        added = sems("added", LAYERS)
        dve_moe = sems("dve_moe", LAYERS)

        n_ret = [RET, 0]
        n_items = [n_ret[l] + HEADS[l] for l in range(LAYERS)]
        n_rot = [ROTATED[l] * T for l in range(LAYERS)]

        block = ctx.enter_context(nc.Block())

        @block.sync
        def _(sp):
            gate_rows = w_gate.rearrange("l e (p c) n -> (l e) p (c n)", c=C)
            up_rows = w_up.rearrange("l e (p c) n -> (l e) p (c n)", c=C)
            down_rows = w_down.rearrange("l e (j p) n -> (l e) p j n", p=P)

            def load_group(l, r, g, experts, first_expert, after_attention=False):
                for k in range(experts):
                    if after_attention:
                        sp.wait_ge(proj_done[l], 2 * T * (k + 1))
                    else:
                        sp.wait_ge(gate_up_done[l], gu_count(r, g, k) - GE)
                    row = l * EXPERTS + first_expert + k
                    sp.dma_start(ring[:, 2 * k, :], gate_rows[row]).then_inc(e_arrived[l][2 * k], 16)
                    sp.dma_start(ring[:, 2 * k + 1, :], up_rows[row]).then_inc(e_arrived[l][2 * k + 1], 16)
                def load_down(k):
                    row = l * EXPERTS + first_expert + k
                    sp.dma_start(ring[:, 6 + k, :].rearrange("p (j n) -> p j n", j=HID // P),
                                 down_rows[row]).then_inc(e_arrived[l][6 + k], 16)

                if after_attention:
                    sp.wait_ge(s_done[l], n_items[l])
                    load_w_out(l, 1)
                    load_down(2)
                    for k in range(2):
                        sp.wait_ge(mixed[l], T * (k + 1))
                        load_down(k)
                else:
                    sp.wait_ge(down_done[l], group_no(r, g))
                    for k in range(experts):
                        load_down(k)

            def load_w_out(l, n):
                sp.dma_start(ring[:, 6 + n, :].rearrange("p (c n) -> p c n", c=C),
                             w_out[l][0].rearrange("(c p) n -> p c n", p=P)[:, :, 512 * n:512 * n + 512])\
                  .then_inc(w_arrived[l][6 + n], 16)

            def load_round(l, r, after_attention=False):
                if after_attention:
                    load_group(l, r, 0, GE, 0, after_attention)
                with sp.Fori(int(after_attention), FULL) as g:
                    load_group(l, r, g, GE, g * GE)
                load_group(l, r, FULL, TAIL, FULL * GE)

            for t in range(T):
                sp.dma_start(h[:, t, :], x[0, P * t:P * t + P, :]).then_inc(x_loaded[t], 16)
            sp.dma_start(cst[:, 0:FIRST_CONSTS], consts[:, 0:FIRST_CONSTS]).then_inc(const_loaded[0], 16)
            for l in range(LAYERS):
                for i, g in ((2 * l, mix[l][0]), (2 * l + 1, ffn_norm[l])):
                    sp.dma_start(gains[:, i, :], g.rearrange("(p c) -> p c", c=C)).then_inc(gain_loaded, 16)
            more = None
            for l in range(LAYERS):
                w_in_v = w_in[l][0].rearrange("(p c) n -> p c n", c=C)
                for j in range(NW):
                    if l:
                        sp.wait_ge(gate_up_done[l - 1],
                                   gu_count(more, FULL, j // 2))
                    b = BLOCKS[l][j]
                    sp.dma_start(ring[:, j, :].rearrange("p (c n) -> p c n", c=C),
                                 w_in_v[:, :, 512 * b:512 * b + 512]).then_inc(w_arrived[l][j], 16)
                    if l == 0 and j == 2:
                        sp.dma_start(cst[:, FIRST_CONSTS:], consts[:, FIRST_CONSTS:]).then_inc(const_loaded[1], 16)
                if l:
                    sp.wait_ge(down_done[l - 1], group_no(more, FULL) + 1)
                load_w_out(l, 0)
                if l == 0:
                    for m in range(LAYERS):
                        for dst, src in ((w_rt[:, m, :, 0:GROUPS], w_group[m].rearrange("(p c) e -> p c e", c=C)),
                                         (w_rt[:, m, :, GROUPS:], w_fine[m].rearrange("(p c) e -> p c e", c=C)),
                                         (b_rt[:, m, 0:GROUPS], b_group[m].partition_broadcast(P)),
                                         (b_rt[:, m, GROUPS:], b_fine[m].partition_broadcast(P))):
                            sp.dma_start(dst, src).then_inc(router_loaded, 16)
                load_round(l, 0, after_attention=True)
                sp.wait_ge(rounds_ready[l], 1)
                more = sp.value_load(rounds_i[0:1, l:l + 1], min_val=0, max_val=MAX_ROUNDS - 1)
                with sp.If(more > 0):
                    with sp.Fori(1, more + 1) as r:
                        load_round(l, r)
            sp.wait_ge(xn_ready, 4 * T + T)
            sp.dma_start(out[0].rearrange("(t p) d -> p t d", p=P), xn_t).then_inc(out_stored, 16)
            sp.wait_ge(out_stored, 16)

        @block.gpsimd
        def _(pool):
            pool.memset(half_exp, -0.5).then_inc(pow_ready, 1)
            pool.wait_ge(pow_ready, 1)

            def rsqrt_norm(ph):
                for t in range(T):
                    pool.wait_ge(var_ready, T * ph + t + 1)
                    pool.tensor_tensor(rstd[:, t:t + 1], var[:, t:t + 1], half_exp[:, 0:1], ALU.pow).then_inc(pow_ready, 1)

            for l in range(LAYERS):
                rsqrt_norm(2 * l)
                pairs = kT.rearrange("p (a b) s -> p a b s", b=2)
                pool.wait_ge(pow_ready, 1 + T * (2 * l + 1))
                pool.memset(pairs[HEAD:P, :, 0, :], 0.0).then_inc(k_cleared[l], 1)
                pool.wait_ge(k_cleared[l], 1)
                pool.memset(pairs[0:HEAD, :, 1, :], 0.0).then_inc(k_cleared[l], 1)
                pool.wait_ge(k_cleared[l], 2)
                for m in range(HEADS[l]):
                    if l == 0 and m == 3:
                        pool.wait_ge(ret_var, 1)
                        pool.tensor_tensor(rrstd, rvar, half_exp[:, 0:1].broadcast_to([P, 8]),
                                           ALU.pow).then_inc(ret_pow, 1)
                    pool.wait_ge(den_ready[l], m + 1)
                    b = prob[(n_ret[l] + m) % 4].rearrange("p (b s) -> p b s", b=3)
                    pool.tensor_tensor(b, b, rden[:, m, :].unsqueeze(2).broadcast_to([P, 3, P]), ALU.mult)\
                        .then_inc(p_ready[l], 1)
                rsqrt_norm(2 * l + 1)
            rsqrt_norm(2 * LAYERS)

        @block.scalar
        def _(act):
            def square(ph, t, half):
                act.activation(xn_t[:, t, 512 * half:512 * half + 512], h[:, t, 512 * half:512 * half + 512],
                               ACT.Square, accum_out=sq[:, t, half:half + 1]).then_inc(squared, 1)

            for t in range(T):
                act.wait_ge(x_loaded[t], 16)
                for half in range(2):
                    square(0, t, half)

            def copy_qkT(l, s):
                act.wait_ge(rot_turned[l], s + 1)
                j, t = divmod(s, T)
                src = psum[4 + s % 2][:, :].rearrange("p (a s) -> p a s", a=4)
                cols = slice(P * t, P * t + P)
                if l == 0:
                    q_pairs, k_pairs = (((0, 4), None), (None, (0, 4)), ((4, 2), (4, 2)))[j]
                else:
                    q_pairs, k_pairs = (((0, 4), None), ((4, 4), None), (None, (0, 4)), (None, (4, 4)))[j]
                if q_pairs:
                    a, n = q_pairs
                    last = act.copy(qT[:, a:a + n, cols], src[:, 0:n, :])
                if k_pairs:
                    a, n = k_pairs
                    if t == 0:
                        act.wait_ge(k_cleared[l], 2)
                    kv = kT.rearrange("p (a b) s -> p a b s", b=2)
                    act.copy(kv[0:HEAD, a:a + n, 0, cols], src[0:HEAD, 4 - n:4, :])
                    last = act.copy(kv[HEAD:P, a:a + n, 1, cols], src[HEAD:P, 4 - n:4, :])
                last.then_inc(qkT_ready[l], 1)

            def exponentials(l, m):
                act.wait_ge(s_out[l], m + 1)
                b = prob[(n_ret[l] + m) % 4]
                for t, cols in ((0, slice(0, P)), (1, slice(P, 3 * P))):
                    sums = {"accum_out": den[:, m, t:t + 1]} if l == 0 else {}
                    last = act.activation(b[:, cols], b[:, cols], ACT.Exp, bias=negm[:, m, t:t + 1], scale=-1.0, **sums)
                last.then_inc(exp_done[l], 1)

            def copy_pT(l, m):
                act.wait_ge(p_turned[l], m + 1)
                if m >= 4:
                    act.wait_ge(pair_done[l], (m - 4) // 2 + 1)
                act.copy(probT[m % 4], psum[2 + m % 2][:, 0:3 * P]).then_inc(pT_ready[l], 1)

            def copy_oT(l, a):
                act.wait_ge(pair_done[l], a + 1)
                act.copy(oT[:, a, :], psum[4 + a % 2][:, 0:SEQ]).then_inc(oT_ready[l], 1)

            def experts_of(l, r, g, n):
                no = group_no(r, g)
                act.wait_ge(gated_turned[l], no + 1)
                act.copy(gatedT[0:SLOTS * n, :], psum[5][0:SLOTS * n, 0:SEQ]).then_inc(gatedT_ready[l], 1)

                def copy_hidT(k):
                    act.wait_ge(hid_turned[l], expert_no(r, g, k) + 1)
                    act.copy(hidT[k], psum[4][:, 0:P]).then_inc(hidT_ready[l], 1)

                for k in range(n):
                    act.wait_ge(gate_up_done[l], gu_count(r, g, k))
                    if k >= 2:
                        act.wait_ge(hid_ready[l], expert_no(r, g, k) - 1)
                    bank = psum[2 + k % 2]
                    act.activation(eg[k % 2], bank[:, 0:P], ACT.Exp, scale=-1.0)
                    act.copy(gu[k % 2], bank[:, 0:2 * P]).then_inc(gate_up_out[l], 1)
                    if k:
                        copy_hidT(k - 1)
                copy_hidT(n - 1)
                act.wait_ge(down_done[l], no + 1)
                act.copy(y_sb[0:SLOTS * n, 0:512], psum[6][0:SLOTS * n, :]).then_inc(y_low[l], 1)

            for l in range(LAYERS):
                for s in range(NW * T + 2):
                    j, t = divmod(s, T)
                    if n_rot[l] <= s < NW * T:
                        act.wait_ge(proj_done[l], s + 1)
                        if l == 0 and j == NW - 1:
                            act.activation(rg[:, t, :], psum[s % 4][:, :], ACT.Exp, scale=-1.0).then_inc(rg_exp, 1)
                        else:
                            at = 512 * (j - ROTATED[l])
                            act.copy(v_sb[:, t, at:at + 512], psum[s % 4][:, :]).then_inc(bank_out[l][s % 4], 1)
                    if 0 <= s - 2 < n_rot[l]:
                        copy_qkT(l, s - 2)
                for i in range(HEADS[l] + 7):
                    if i < HEADS[l]:
                        exponentials(l, i)
                    if 0 <= i - 3 < HEADS[l]:
                        copy_pT(l, i - 3)
                    if 0 <= i - 6 < HEADS[l] and i % 2:
                        copy_oT(l, (i - 6) // 2)
                if l == 0:
                    for t in range(T):
                        act.wait_ge(ret_turned, t + 1)
                        act.copy(oT[:, 4:8, P * t:P * t + P], psum[6 + t][:, :].rearrange("p (a s) -> p a s", a=4))\
                           .then_inc(retT_ready, 1)
                for n in range(2):
                    for t in range(T):
                        act.wait_ge(mix_added[l], 2 * n + t + 1)
                        square(2 * l + 1, t, n)
                act.wait_ge(gmax_ready[l], 1)
                for t in range(T):
                    act.activation(expg[:, t, :], lg[:, t, 0:GROUPS], ACT.Exp, bias=gv[:, t:t + 1],
                                   accum_out=gv[:, 2 + t:3 + t])
                act.activation(gv[:, 4:6], gv[:, 6:8], ACT.Exp).then_inc(gexp_done[l], 1)
                if l == LAYERS - 1:
                    act.dma_start(gain_row, final_norm.partition_broadcast(P)).then_inc(fin_loaded, 16)
                act.wait_ge(rounds_ready[l], 1)
                more = act.value_load(rounds_i[0:1, l:l + 1], min_val=0, max_val=MAX_ROUNDS - 1)
                with act.Fori(0, more + 1) as r:
                    with act.Fori(0, FULL) as g:
                        experts_of(l, r, g, GE)
                    experts_of(l, r, FULL, TAIL)
                for q in range(4):
                    act.wait_ge(added[l], group_no(more, FULL) * 4 + (q + 1))
                    square(2 * l + 2, *divmod(q, 2))

        @block.tensor
        def _(pe):
            pe.wait_ge(const_loaded[0], 16)

            def turn_xn(ph, t):
                pe.wait_ge(xn_ready, ph * T + t + 1)
                for q in range(2):
                    for c in range(4):
                        last = pe.transpose(psum[2 * t + q][:, P * c:P * c + P], xn_c[:, t, 4 * q + c, :], ident)
                    last.then_inc(xn_turned, 1)

            def project(l, s):
                j, t = divmod(s, T)
                pe.wait_ge(w_arrived[l][j], 16)
                if s < T:
                    pe.wait_ge(xnT_ready, 4 * (2 * l) + 4)
                if s >= 4:
                    pe.wait_ge(bank_out[l][s % 4], s // 4)
                for c in range(C):
                    last = pe.matmul(psum[s % 4][:, :], xnT[:, c, P * t:P * t + P],
                                     ring[:, j, 512 * c:512 * c + 512], start=(c == 0), stop=(c == C - 1))
                last.then_inc(proj_done[l], 1)

            def turn_rot(l, s):
                pe.wait_ge(rot_ready[l], s + 1)
                if s >= 2:
                    pe.wait_ge(qkT_ready[l], s - 1)
                for a in range(4):
                    last = pe.transpose(psum[4 + s % 2][:, P * a:P * a + P], rot[s % 3][:, P * a:P * a + P], ident)
                last.then_inc(rot_turned[l], 1)

            def scores(l, i):
                before = i - 2
                if 0 <= before < n_ret[l]:
                    pe.wait_ge(ret_ready, before + 1)
                elif before >= 0:
                    pe.wait_ge(s_out[l], before - n_ret[l] + 1)
                bank = psum[i % 2]
                if i < n_ret[l]:
                    q, k = qT[:, 4 + i // 2, :], kT[:, HEADS[l] + i, :]
                    pe.matmul(bank[:, 0:2 * P], k[:, 0:P], q, start=True, stop=True)
                    last = pe.matmul(bank[:, 2 * P:3 * P], k[:, P:SEQ], q[:, P:SEQ], start=True, stop=True)
                else:
                    m = i - n_ret[l]
                    q, k = qT[:, m // 2, :], kT[:, m, :]
                    pe.matmul(bank[:, 0:P], q[:, 0:P], k[:, 0:P], start=True, stop=True)
                    last = pe.matmul(bank[:, P:3 * P], q[:, P:SEQ], k, start=True, stop=True)
                last.then_inc(s_done[l], 1)

            def retain(n):
                pe.wait_ge(ret_ready, n + 1)
                w = prob[n]
                for t, b, kt in ((0, 0, 0), (1, 1, 0), (1, 2, 1)):
                    last = pe.matmul(psum[6 + t][:, P * n:P * n + P], w[:, P * b:P * b + P],
                                     v_sb[:, kt, 512 + P * n:512 + P * n + P], start=(kt == 0), stop=(t == kt))
                last.then_inc(ret_done, 1)

            def turn_p(l, m):
                pe.wait_ge(p_ready[l], m + 1)
                if m >= 2:
                    pe.wait_ge(pT_ready[l], m - 1)
                b4 = prob[(n_ret[l] + m) % 4]
                for b in range(3):
                    last = pe.transpose(psum[2 + m % 2][:, P * b:P * b + P], b4[:, P * b:P * b + P], ident)
                last.then_inc(p_turned[l], 1)

            def values(l, a):
                pe.wait_ge(pT_ready[l], 2 * a + 2)
                if a >= 2:
                    pe.wait_ge(oT_ready[l], a - 1)
                bank = psum[4 + a % 2]
                for kt in range(T):
                    for m in (2 * a, 2 * a + 1):
                        lo = HEAD * (m % 2)
                        cols = slice(P * kt, SEQ)
                        pT = probT[m % 4][:, 0:SEQ] if kt == 0 else probT[m % 4][:, SEQ:SEQ + P]
                        last = pe.matmul(bank[lo:lo + HEAD, cols], v_sb[:, kt, HEAD * m:HEAD * m + HEAD], pT,
                                         start=(kt == 0), stop=(kt == T - 1), tile_position=(0, lo))
                last.then_inc(pair_done[l], 1)

            def experts_of(l, r, g, n):
                no = group_no(r, g)
                rows = SLOTS * n
                pe.wait_ge(onehot_ready[l], no + 1)
                for t in range(T):
                    last = pe.transpose(psum[5][0:SLOTS * GE, P * t:P * t + P],
                                        gated[:, t, :, :].rearrange("p k s -> p (k s)"), ident)
                last.then_inc(gated_turned[l], 1)
                for c in range(C):
                    for t in range(T):
                        last = pe.matmul(psum[c // 4][:, rows * (c % 4):rows * (c % 4) + rows],
                                         xn_c[:, t, c, :], onehot[:, t, 0:n, :].rearrange("p k s -> p (k s)"),
                                         start=(t == 0), stop=(t == T - 1))
                    if c % 4 == 3:
                        last.then_inc(gathered[l], 1)
                pe.wait_ge(xT_ready[l], no * 2 + 2)

                def turn_hid(k):
                    e = expert_no(r, g, k)
                    pe.wait_ge(hid_ready[l], e + 1)
                    if k:
                        pe.wait_ge(hidT_ready[l], e)
                    pe.transpose(psum[4][:, 0:P], hid[k % 2], ident).then_inc(hid_turned[l], 1)

                for k in range(n):
                    e = expert_no(r, g, k)
                    if k >= 2:
                        pe.wait_ge(gate_up_out[l], e - 1)
                    pe.wait_ge(e_arrived[l][2 * k], arrivals(2 * k, r, g))
                    pe.wait_ge(e_arrived[l][2 * k + 1], arrivals(2 * k + 1, r, g))
                    bank = psum[2 + k % 2]
                    for c in range(C):
                        for j in range(4):
                            last = pe.matmul(
                                bank[32 * j:32 * j + 32, 0:2 * P].rearrange("p (a s) -> p a s", a=2),
                                xT[:, c, SLOTS * k:SLOTS * k + SLOTS],
                                ring[:, 2 * k:2 * k + 2, 512 * c + P * j:512 * c + P * j + P],
                                start=(c == 0), stop=(c == C - 1), tile_position=(0, 32 * j))
                    last.then_inc(gate_up_done[l], 1 if n == GE or k < n - 1 else 1 + GE - n)
                    if k:
                        turn_hid(k - 1)
                turn_hid(n - 1)
                for k in range(n):
                    pe.wait_ge(e_arrived[l][6 + k], arrivals(6 + k, r, g))
                pe.wait_ge(hidT_ready[l], expert_no(r, g, n))
                for j in range(HID // P):
                    for half in range(2):
                        for k in range(n):
                            last = pe.matmul(
                                psum[6 + half][32 * k:32 * k + 32, :], hidT[k][:, 32 * j:32 * j + 32],
                                ring[:, 6 + k, D * j + 512 * half:D * j + 512 * half + 512],
                                start=(j == 0), stop=(j == HID // P - 1), tile_position=(0, 32 * k))
                last.then_inc(down_done[l], 1)
                pe.wait_ge(y_low[l], no + 1)
                pe.wait_ge(y_high[l], no + 1)
                pe.wait_ge(gatedT_ready[l], no + 1)
                for q in range(4):
                    t, half = divmod(q, 2)
                    if q >= 2:
                        pe.wait_ge(added[l], no * 4 + (q - 1))
                    pe.matmul(psum[q % 2][:, :], gatedT[0:rows, P * t:P * t + P],
                              y_sb[0:rows, 512 * half:512 * half + 512], start=True, stop=True)\
                      .then_inc(scattered[l], 1)

            for l in range(LAYERS):
                for t in range(T):
                    turn_xn(2 * l, t)
                for s in range(NW * T + 2):
                    if s < NW * T:
                        project(l, s)
                    if 0 <= s - 2 < n_rot[l]:
                        turn_rot(l, s - 2)
                pe.wait_ge(qkT_ready[l], n_rot[l])
                for b in range(4):
                    pe.wait_ge(bank_out[l][b], 3)
                if l == 0:
                    pe.wait_ge(const_loaded[1], 16)
                for i in range(n_items[l] + 6):
                    m = i - n_ret[l]
                    if i < n_items[l]:
                        scores(l, i)
                    if 0 <= i - 2 < n_ret[l]:
                        retain(i - 2)
                    if 0 <= m - 3 < HEADS[l]:
                        turn_p(l, m - 3)
                    if 0 <= m - 5 < HEADS[l] and (m - 5) % 2:
                        values(l, (m - 5) // 2)
                if l == 0:
                    for t in range(T):
                        pe.wait_ge(ret_normed, t + 1)
                        for c in range(4):
                            last = pe.transpose(psum[6 + t][:, P * c:P * c + P], o_ret[:, t, P * c:P * c + P], ident)
                        last.then_inc(ret_turned, 1)
                    pe.wait_ge(retT_ready, T)
                pe.wait_ge(oT_ready[l], HEADS[l] // 2)
                for n in range(2):
                    pe.wait_ge(w_arrived[l][6 + n], 16)
                    for t in range(T):
                        for c in range(C):
                            last = pe.matmul(psum[4 + 2 * n + t][:, :], oT[:, c, P * t:P * t + P],
                                             ring[:, 6 + n, 512 * c:512 * c + 512], start=(c == 0), stop=(c == C - 1))
                        last.then_inc(mixed[l], 1)
                pe.wait_ge(router_loaded, 8 * 16)
                for t in range(T):
                    turn_xn(2 * l + 1, t)
                    pe.wait_ge(xnT_ready, 4 * (2 * l + 1) + 2 * t + 2)
                    for c in range(C):
                        last = pe.matmul(psum[4 + t][:, 0:36], xnT[:, c, P * t:P * t + P],
                                         w_rt[:, l, c, :], start=(c == 0), stop=(c == C - 1))
                    last.then_inc(logits_done[l], 1)
                pe.wait_ge(assigned[l], 1)
                before, ones = const("before"), const("ones")
                pe.matmul(psum[6][:, 0:32], before, asg[:, 0, :], start=True, stop=True)
                pe.matmul(psum[6][:, 32:64], ones, asg[:, 0, :], start=True, stop=False)
                pe.matmul(psum[6][:, 32:64], before, asg[:, 1, :], start=False, stop=True)
                pe.matmul(psum[6][:, 64:96], ones, asg[:, 0, :], start=True, stop=False)
                pe.matmul(psum[6][:, 64:96], ones, asg[:, 1, :], start=False, stop=True).then_inc(pos_done[l], 1)
                pe.wait_ge(rounds_ready[l], 1)
                more = pe.value_load(rounds_i[0:1, l:l + 1], min_val=0, max_val=MAX_ROUNDS - 1)
                with pe.Fori(0, more + 1) as r:
                    with pe.Fori(0, FULL) as g:
                        experts_of(l, r, g, GE)
                    experts_of(l, r, FULL, TAIL)

        @block.vector
        def _(dve):
            norm_link = Chain(dve, dve_norm).link

            def scale_rows(ph, t, squares):
                link = norm_link
                one = slice(t, t + 1)
                dve.wait_ge(squared, 4 * ph + squares)
                link(dve.tensor_tensor(sumsq[:, one], sq[:, t, 0:1], sq[:, t, 1:2], ALU.add))
                dve.tensor_scalar(var[:, one], sumsq[:, one], 1.0 / D, EPS, ALU.mult, ALU.add).then_inc(var_ready, 1)
                dve.wait_ge(pow_ready, T * ph + t + 2)
                link(dve.scalar_tensor_tensor(out=newt[:, one], in0=rstd[:, one], scalar=var[:, one],
                                              in1=rstd[:, one], op0=ALU.mult, op1=ALU.mult))
                link(dve.tensor_scalar(newt[:, one], newt[:, one], -0.5, 1.5, ALU.mult, ALU.add))
                link(dve.tensor_tensor(rstd[:, one], rstd[:, one], newt[:, one], ALU.mult))
                if ph < 2 * LAYERS:
                    dve.tensor_scalar(xn_c[:, t, :, :], h[:, t, :].rearrange("p (q c) -> p c q", c=C),
                                      rstd[:, one], None, ALU.mult).then_inc(xn_ready, 1)
                else:
                    dve.scalar_tensor_tensor(out=xn_t[:, t, :], in0=h[:, t, :], scalar=rstd[:, one],
                                             in1=gain_row, op0=ALU.mult, op1=ALU.mult).then_inc(xn_ready, 1)

            def gain_columns(ph, t):
                for q in range(2):
                    dve.wait_ge(xn_turned, 4 * ph + 2 * t + q + 1)
                    dve.tensor_tensor(xnT[:, 4 * q:4 * q + 4, P * t:P * t + P],
                                      psum[2 * t + q][:, :].rearrange("p (a s) -> p a s", a=4),
                                      gains[:, ph, 4 * q:4 * q + 4].unsqueeze(2).broadcast_to([P, 4, P]),
                                      ALU.mult).then_inc(xnT_ready, 1)

            def rotate(l, s, link):
                j, t = divmod(s, T)
                dve.wait_ge(proj_done[l], s + 1)
                if s >= 3:
                    dve.wait_ge(rot_turned[l], s - 2)
                kind = "ret" if l == 0 and j == 2 else "rope"
                form = "p (h d x) -> p h d x" if kind == "ret" else "p (h x d) -> p h x d"

                def halves(ap, n):
                    v = ap.rearrange(form, h=n, x=2)
                    return (v[:, :, :, 0], v[:, :, :, 1]) if kind == "ret" else (v[:, :, 0, :], v[:, :, 1, :])

                cos = const(kind + "_cos", T, HEAD)[:, t, :]
                sin = const(kind + "_sin", T, HEAD)[:, t, :]
                bank = psum[s % 4][:, :]
                dve.tensor_tensor(rot[s % 3].rearrange("p (h d) -> p h d", h=8),
                                  bank.rearrange("p (h d) -> p h d", h=8),
                                  cos.unsqueeze(1).broadcast_to([P, 8, HEAD]), ALU.mult)
                src, dst, sn = halves(bank, 8), halves(rot_tmp, 8), halves(sin, 1)
                for a in range(2):
                    last = dve.tensor_tensor(dst[a], src[1 - a], sn[a].broadcast_to([P, 8, HEAD // 2]), ALU.mult)
                last.then_inc(bank_out[l][s % 4], 1)
                dve.wait_ge(bank_out[l][s % 4], s // 4 + 1)
                dve.tensor_tensor(rot[s % 3], rot[s % 3], rot_tmp, ALU.add).then_inc(rot_ready[l], 1)
                dve.wait_ge(rot_ready[l], s + 1)

            def head_max(l, m):
                i = n_ret[l] + m
                dve.wait_ge(s_done[l], i + 1)
                if m >= 4:
                    dve.wait_ge(p_turned[l], m - 3)
                elif l == 0:
                    dve.wait_ge(ret_done, m + 1)
                mask = const("mask0" if l == 0 else "mask1")
                for t, cols in ((0, slice(0, P)), (1, slice(P, 3 * P))):
                    last = dve.tensor_tensor_reduce(prob[i % 4][:, cols], psum[i % 2][:, cols], mask[:, cols],
                                                    -(HEAD ** -0.5), FAR, ALU.add, ALU.min, negm[:, m, t:t + 1])
                last.then_inc(s_out[l], 1)

            def head_sum(l, m, link):
                dve.wait_ge(exp_done[l], m + 1)
                if l == 1:
                    b, count = prob[m % 4], const("count1")
                    for t, cols in ((0, slice(0, P)), (1, slice(P, 3 * P))):
                        last = dve.tensor_tensor_reduce(b[:, cols], b[:, cols], count[:, cols],
                                                        1.0, 0.0, ALU.mult, ALU.add, den[:, m, t:t + 1])
                    link(last)
                dve.reciprocal(rden[:, m, 0:2], den[:, m, :])
                dve.reciprocal(rden[:, m, 2:3], den[:, m, 1:2]).then_inc(den_ready[l], 1)

            def decayed(n):
                dve.wait_ge(s_done[0], n + 1)
                dk = const("decay", RET, 2 * P)[:, n, :]
                dve.tensor_tensor(prob[n][:, 0:2 * P], psum[n % 2][:, 0:2 * P], dk, ALU.mult)
                dve.tensor_tensor(prob[n][:, 2 * P:3 * P], psum[n % 2][:, 2 * P:3 * P], dk[:, 0:P],
                                  ALU.mult).then_inc(ret_ready, 1)

            def retention_variance(link):
                dve.wait_ge(ret_done, RET)
                for t in range(T):
                    for n in range(RET):
                        last = dve.bn_stats(bnst[:, RET * t + n, :], psum[6 + t][:, P * n:P * n + P])
                link(last)
                for t in range(T):
                    for n in range(RET):
                        last = dve.bn_aggr(rstat[:, t, n, :], bnst[:, RET * t + n, :])
                link(last)
                dve.tensor_scalar(rvar.rearrange("p (t h) -> p t h", t=T), rstat[:, :, :, 1], EPS, None, ALU.add)\
                   .then_inc(ret_var, 1)

            def retention_norm(link):
                dve.wait_ge(ret_pow, 1)
                step = small[:, 258:266]
                link(dve.tensor_tensor(step, rrstd, rrstd, ALU.mult))
                link(dve.tensor_tensor(step, step, rvar, ALU.mult))
                link(dve.tensor_scalar(step, step, -0.5, 1.5, ALU.mult, ALU.add))
                link(dve.tensor_tensor(rrstd, rrstd, step, ALU.mult))
                for t in range(T):
                    for n in range(RET):
                        m = RET * t + n
                        last = dve.tensor_scalar(o_ret[:, t, P * n:P * n + P], psum[6 + t][:, P * n:P * n + P],
                                                 rstat[:, t, n, 0:1], rrstd[:, m:m + 1], ALU.subtract, ALU.mult)
                    link(last)
                    dve.tensor_tensor(o_ret[:, t, :], o_ret[:, t, :], rg[:, t, :], ALU.mult).then_inc(ret_normed, 1)

            def route(l, link):
                dve.wait_ge(logits_done[l], T)
                for t in range(T):
                    link(dve.memset(lg[:, t, :], -FAR))
                for t in range(T):
                    logits, bias = psum[4 + t], b_rt[:, l, :]
                    dve.tensor_tensor(lg[:, t, 0:GROUPS], logits[:, 0:GROUPS], bias[:, 0:GROUPS], ALU.add)
                    last = dve.tensor_tensor(lf[:, t, :], logits[:, GROUPS:36], bias[:, GROUPS:36], ALU.add)
                link(last)
                for t in range(T):
                    link(dve.max(top[:, t, :], lg[:, t, :]))
                for t in range(T):
                    last = dve.max_index(idx_u[:, t, :], top[:, t, :], lg[:, t, :])
                link(last)
                link(dve.tensor_copy(idx[:, 0:2], idx_u[:, 0:2, 0]))
                dve.tensor_scalar(gv[:, 0:2], top[:, 0:2, 0], -1.0, None, ALU.mult)
                for t in range(T):
                    last = dve.tensor_scalar(gmask[:, t, :], const("iota")[:, 0:GROUPS], idx[:, t:t + 1], None,
                                             ALU.is_equal)
                link(last)
                link(dve.tensor_scalar(pen, gmask, FAR, -FAR, ALU.mult, ALU.add))
                by_group = "p (g e) -> p g e"
                for t in range(T):
                    m, f = masked[:, t, :].rearrange(by_group, g=GROUPS), lf[:, t, :].rearrange(by_group, g=GROUPS)
                    link(dve.tensor_tensor(m, f, gmask[:, t, :].unsqueeze(2).broadcast_to([P, GROUPS, 8]), ALU.mult))
                    link(dve.tensor_tensor(m, m, pen[:, t, :].unsqueeze(2).broadcast_to([P, GROUPS, 8]), ALU.add))
                for t in range(T):
                    link(dve.max(top[:, T + t, :], masked[:, t, :]))
                for t in range(T):
                    last = dve.max_index(idx_u[:, T + t, :], top[:, T + t, :], masked[:, t, :])
                link(last)
                dve.tensor_copy(idx[:, 2:4], idx_u[:, 2:4, 0])
                link(dve.tensor_copy(idx[:, 4:6], idx_u[:, 2:4, 1]))
                dve.tensor_tensor(gv[:, 6:8], top[:, 2:4, 1], top[:, 2:4, 0], ALU.subtract).then_inc(gmax_ready[l], 1)
                for t in range(T):
                    dve.tensor_scalar(first[:, t, :], const("iota"), idx[:, 2 + t:3 + t], None, ALU.is_equal)
                    last = dve.tensor_scalar(second[:, t, :], const("iota"), idx[:, 4 + t:5 + t], None, ALU.is_equal)
                link(last)
                dve.tensor_tensor(asg[:], first, second, ALU.add).then_inc(assigned[l], 1)
                dve.wait_ge(gexp_done[l], 1)
                link(dve.tensor_scalar(gv[:, 8:10], gv[:, 4:6], 1.0, None, ALU.add))
                link(dve.tensor_tensor(gv[:, 8:10], gv[:, 8:10], gv[:, 2:4], ALU.mult))
                link(dve.reciprocal(gv[:, 10:12], gv[:, 8:10]))
                link(dve.tensor_tensor(gv[:, 12:14], gv[:, 10:12], gv[:, 4:6], ALU.mult))
                for t in range(T):
                    link(dve.tensor_scalar(gate[:, t, 0:EXPERTS], first[:, t, :], gv[:, 10 + t:11 + t], None, ALU.mult))
                    link(dve.scalar_tensor_tensor(out=gate[:, t, 0:EXPERTS], in0=second[:, t, :],
                                                  scalar=gv[:, 12 + t:13 + t], in1=gate[:, t, 0:EXPERTS],
                                                  op0=ALU.mult, op1=ALU.add))
                dve.wait_ge(pos_done[l], 1)
                pos = psum[6][:, 0:64].rearrange("p (t e) -> p t e", t=T)
                link(dve.scalar_tensor_tensor(out=posm[:, :, 0:EXPERTS], in0=pos, scalar=1.0, in1=asg[:],
                                              op0=ALU.add, op1=ALU.mult))
                link(dve.tensor_scalar(posm[:, :, 0:EXPERTS], posm[:, :, 0:EXPERTS], -1.0, None, ALU.add))
                link(dve.reduce_max(cnt[:, 0:1], psum[6][:, 64:96], AX.X))
                link(dve.tensor_scalar(limhit[:], const("limits"), cnt[:, 0:1], None, ALU.is_lt))
                link(dve.reduce_sum(rounds_f[:, 0:1], limhit[:], AX.X))
                dve.tensor_scalar(rounds_i[:, l:l + 1], rounds_f[:, 0:1], -1.0, None, ALU.add)\
                   .then_inc(rounds_ready[l], 1)

            def experts_of(l, r, g, n, first_expert, base):
                chain = Chain(dve, dve_moe[l], base)
                no = group_no(r, g)
                cols = bass.ds(first_expert, n)
                chain.link(dve.tensor_tensor(
                    onehot[:, :, 0:n, :], const("iota").unsqueeze(1).unsqueeze(1).broadcast_to([P, T, n, SLOTS]),
                    posm[:, :, cols].unsqueeze(3).broadcast_to([P, T, n, SLOTS]), ALU.is_equal))
                dve.tensor_tensor(gated[:, :, 0:n, :], onehot[:, :, 0:n, :],
                                  gate[:, :, cols].unsqueeze(3).broadcast_to([P, T, n, SLOTS]), ALU.mult)\
                   .then_inc(onehot_ready[l], 1)
                for q in range(2):
                    dve.wait_ge(gathered[l], no * 2 + (q + 1))
                    dve.tensor_tensor(xT[:, 4 * q:4 * q + 4, 0:SLOTS * n],
                                      psum[q][:, 0:4 * SLOTS * n].rearrange("p (a s) -> p a s", a=4),
                                      gains[:, 2 * l + 1, 4 * q:4 * q + 4].unsqueeze(2).broadcast_to([P, 4, SLOTS * n]),
                                      ALU.mult).then_inc(xT_ready[l], 1)
                for k in range(n):
                    e = expert_no(r, g, k)
                    dve.wait_ge(gate_up_out[l], e + 1)
                    if k >= 2:
                        dve.wait_ge(hid_turned[l], e - 1)
                    eb, gb = eg[k % 2], gu[k % 2]
                    chain.link(dve.tensor_scalar(eb, eb, 1.0, None, ALU.add))
                    chain.link(dve.reciprocal(eb, eb))
                    chain.link(dve.tensor_tensor(eb, eb, gb[:, 0:P], ALU.mult))
                    dve.tensor_tensor(hid[k % 2], eb, gb[:, P:2 * P], ALU.mult).then_inc(hid_ready[l], 1)
                dve.wait_ge(down_done[l], no + 1)
                dve.tensor_copy(y_sb[0:SLOTS * n, 512:1024], psum[7][0:SLOTS * n, :]).then_inc(y_high[l], 1)
                for q in range(4):
                    t, half = divmod(q, 2)
                    dve.wait_ge(scattered[l], no * 4 + (q + 1))
                    hv = h[:, t, 512 * half:512 * half + 512]
                    dve.tensor_tensor(hv, hv, psum[q % 2][:, :], ALU.add).then_inc(added[l], 1)
                return chain.n

            for l in range(LAYERS):
                link = Chain(dve, dve_attn[l]).link
                for t in range(T):
                    scale_rows(2 * l, t, 2 * t + 2)
                dve.wait_ge(gain_loaded, 4 * 16)
                for t in range(T):
                    gain_columns(2 * l, t)
                dve.wait_ge(const_loaded[0], 16)
                for s in range(n_rot[l]):
                    rotate(l, s, link)
                if l == 0:
                    for t in range(T):
                        s = (NW - 1) * T + t
                        dve.wait_ge(rg_exp, t + 1)
                        link(dve.tensor_scalar(rg[:, t, :], rg[:, t, :], 1.0, None, ALU.add))
                        link(dve.reciprocal(rg[:, t, :], rg[:, t, :]))
                        dve.tensor_tensor(rg[:, t, :], rg[:, t, :], psum[s % 4][:, :], ALU.mult)\
                           .then_inc(bank_out[l][s % 4], 1)
                    dve.wait_ge(const_loaded[1], 16)
                for n in range(n_ret[l]):
                    decayed(n)
                for m in range(HEADS[l] + 1):
                    if m < HEADS[l]:
                        head_max(l, m)
                    if m:
                        head_sum(l, m - 1, link)
                    if l == 0 and m == 3:
                        retention_variance(link)
                    if l == 0 and m == 5:
                        retention_norm(link)
                for n in range(2):
                    for t in range(T):
                        dve.wait_ge(mixed[l], 2 * n + t + 1)
                        hv = h[:, t, 512 * n:512 * n + 512]
                        dve.tensor_tensor(hv, hv, psum[4 + 2 * n + t][:, :], ALU.add).then_inc(mix_added[l], 1)
                        if n == 1:
                            scale_rows(2 * l + 1, t, 3 + t)
                for t in range(T):
                    gain_columns(2 * l + 1, t)
                route_chain = Chain(dve, dve_route[l])
                route(l, route_chain.link)
                dve.wait_ge(rounds_ready[l], 1)
                more = dve.value_load(rounds_i[0:1, l:l + 1], min_val=0, max_val=MAX_ROUNDS - 1)
                with dve.Fori(0, more + 1) as r:
                    with dve.Fori(0, FULL) as g:
                        n = experts_of(l, r, g, GE, g * GE, r * DVE_ROUND + g * DVE_GROUP)
                        assert n == DVE_GROUP
                    base = r * DVE_ROUND + FULL * DVE_GROUP
                    n = experts_of(l, r, FULL, TAIL, FULL * GE, base)
                    chain = Chain(dve, dve_moe[l], base + n)
                    chain.link(dve.tensor_scalar(posm[:, :, 0:EXPERTS], posm[:, :, 0:EXPERTS], -float(SLOTS), None,
                                                 ALU.add))
                    assert FULL * DVE_GROUP + n + 1 == DVE_ROUND
            dve.wait_ge(fin_loaded, 16)
            for t in range(T):
                scale_rows(2 * LAYERS, t, 2 * t + 2)


_INS = ['x', 'mix_norm_even', 'w_in_even', 'w_out_even', 'mix_norm_odd', 'w_in_odd', 'w_out_odd', 'ffn_norm',
        'w_router_group', 'b_router_group', 'w_router_expert', 'b_router_expert', 'w_expert_gate',
        'w_expert_up', 'w_expert_down', 'final_norm']


def kernel(**inputs):
    import concourse.bacc as _bacc
    from concourse.bass_utils import run_bass_kernel_spmd as _run

    nc = _bacc.Bacc("TRN2", target_bir_lowering=False, num_devices=1)
    arrays, args = {}, []
    for name in _INS:
        a = np.ascontiguousarray(inputs[name])
        arrays[f"in_{name}"] = a
        args.append(nc.dram_tensor(f"in_{name}", a.shape, mybir.dt.from_np(a.dtype), kind="ExternalInput").ap())
    arrays["shape_consts"] = shape_constants()
    args.append(nc.dram_tensor("shape_consts", (P, CONST_COLS), F32, kind="ExternalInput").ap())
    args.append(nc.dram_tensor("out_0", (1, SEQ, D), F32, kind="ExternalOutput").ap())
    build(nc, *args)
    r = _run(nc, [arrays], core_ids=[0])
    return r.results[0]["out_0"]
```

```python
from contextlib import ExitStack

import numpy as np

import concourse.bass as bass
from concourse import mybir

F32 = mybir.dt.float32
F32R = mybir.dt.float32r
I32 = mybir.dt.int32
U32 = mybir.dt.uint32
ALU = mybir.AluOpType
ACT = mybir.ActivationFunctionType
AX = mybir.AxisListType

P = 128
D = 1024
SEQ = 256
T = SEQ // P
C = D // P
LAYERS = 2
HEAD = 64
NW = 6
HEADS = (8, 16)
RET = 4
ROTATED = (3, 4)
BLOCKS = ((0, 1, 3, 5, 2, 4), (0, 1, 2, 3, 4, 5))
MIX_ORDER = ((0, 1, 4, 5, 6, 7, 2, 3), tuple(range(D // P)))
MIX_EARLY = ({1: (0,), 2: (1,), 3: (4, 5)}, {1: (0,), 2: (1,), 3: (2, 3)})
LOGITS_AT = 5
RG = 3
ROTATE_AT = (4, 6)
TURN_AT = (4, 6)
COPY_AT = (6, 8)
PARTS = 4
LAG = 3
EXPERTS = 32
GROUPS = 4
SLOTS = 32
GE = 3
FULL = EXPERTS // GE
TAIL = EXPERTS - FULL * GE
HID = 512
MAX_ROUNDS = SEQ // SLOTS
EPS = 1e-6
FAR = 3.0e38
UNIT = 4096

CONST_WIDTHS = (
    ("ident", P),
    ("rope_cos", T * HEAD), ("rope_sin", T * HEAD), ("ret_cos", T * HEAD), ("ret_sin", T * HEAD),
    ("mask0", 3 * P), ("decay", RET * 2 * P), ("before", P), ("ones", P), ("iota", 33), ("limits", 7),
    ("mask1", 3 * P), ("count1", 3 * P),
)
FIRST_CONSTS = P + 4 * T * HEAD
CONST_AT = {}
_at = 0
for _name, _w in CONST_WIDTHS:
    CONST_AT[_name] = (_at, _w)
    _at += _w
CONST_COLS = _at


def shape_constants():
    f = np.float32
    out = np.zeros((P, CONST_COLS), f)

    def put(name, a):
        at, w = CONST_AT[name]
        out[:, at:at + w] = np.asarray(a, f).reshape(P, w)

    i = np.arange(P)
    put("ident", np.eye(P))
    put("before", i[:, None] < i[None, :])
    put("ones", np.ones((P, P)))
    put("iota", np.tile(np.arange(33), (P, 1)))
    put("limits", np.tile(np.arange(1, MAX_ROUNDS) * SLOTS, (P, 1)))
    q, k = i[:, None], i[None, :]
    causal = np.where(k <= q, 0.0, -1e30)
    put("mask0", np.concatenate([causal, np.zeros((P, P)), causal], 1))

    def windows(dist):
        n = np.zeros(dist.shape)
        for window, dil in ((128, 1), (512, 4), (2048, 16)):
            n += (dist >= 0) & (dist % dil == 0) & (dist // dil <= window // dil)
        return n

    near, far = windows(q - k), windows(q + P - k)
    count = np.concatenate([near, far, near], 1)
    put("count1", count)
    put("mask1", np.where(count > 0, 0.0, -1e30))
    half = HEAD // 2
    pos = np.arange(SEQ, dtype=f)[:, None]
    inv = (f(1.0) / (f(10000.0) ** (np.arange(half, dtype=f) * f(2.0 / HEAD)))).astype(f)
    ang = pos * inv[None, :]
    cos, sin = np.cos(ang).astype(f), np.sin(ang).astype(f)
    tok = lambda a: a.reshape(T, P, -1).transpose(1, 0, 2)
    put("rope_cos", tok(np.concatenate([cos, cos], 1)))
    put("rope_sin", tok(np.concatenate([-sin, sin], 1)))
    freq = (f(1.0) / (f(10000.0) ** np.linspace(0.0, 1.0, half, dtype=f))).astype(f)
    ang = pos * freq[None, :]
    cos, sin = np.cos(ang).astype(f), np.sin(ang).astype(f)
    put("ret_cos", tok(np.stack([cos, cos], -1).reshape(SEQ, HEAD)))
    put("ret_sin", tok(np.stack([-sin, sin], -1).reshape(SEQ, HEAD)))
    rel = np.arange(SEQ)[None, :] - i[:, None]
    decay = []
    for h in range(RET):
        log_gamma = np.log(1.0 - 2.0 ** (-5.0 - h))
        decay.append(np.where(rel >= 0, np.exp(log_gamma * np.maximum(rel, 0)), 0.0) * HEAD ** -0.5)
    put("decay", np.stack(decay, 1))
    return out


class Chain:

    def __init__(self, eng, sem, base=0):
        self.eng, self.sem, self.base, self.n = eng, sem, base, 0

    def link(self, ins):
        self.n += 1
        ins.then_inc(self.sem, 1)
        self.eng.wait_ge(self.sem, self.base + self.n)


def group_no(r, g):
    return r * (FULL + 1) + g


def expert_no(r, g, k):
    return r * EXPERTS + g * GE + k


def gu_count(r, g, k):
    return r * ((FULL + 1) * GE) + g * GE + (k + 1)


def y_rows(n):
    return SLOTS * n if n == GE else 2 * SLOTS * n


def down_no(r, g):
    return r * (FULL + 2) + g


def arrivals(pos, r, g):
    per_round = FULL if pos in (4, 5) else FULL + 1
    return (r * per_round + g + 1) * 16


GATE_STEPS = 4
DVE_GROUP = 3 * GE
DVE_ROUND = FULL * DVE_GROUP + 3 * TAIL + 1


def build(nc, x, mix_even, w_in_even, w_out_even, mix_odd, w_in_odd, w_out_odd, ffn_norm,
          w_group, b_group, w_fine, b_fine, w_gate, w_up, w_down, final_norm, consts, out):
    w_in = (w_in_even, w_in_odd)
    w_out = (w_out_even, w_out_odd)
    mix = (mix_even, mix_odd)
    with ExitStack() as ctx:
        def sb(name, shape, dt=F32):
            return ctx.enter_context(nc.sbuf_tensor(name, shape, dt))

        def sem(name):
            return ctx.enter_context(nc.semaphore(name))

        def sems(name, n):
            return [sem(f"{name}{i}") for i in range(n)]

        def sb_at(name, shape, offset, dt):
            return nc.alloc_sbuf_tensor_at(name, shape, dt, offset=offset)

        def next_place():
            return -(-nc.sbuf_base // 32) * 32

        ring_at = next_place()
        ring = sb("ring", [P, 9, UNIT])
        h = sb("h", [P, T, D])
        xn = sb("xn", [P, T * D])
        hT_at = next_place()
        hT = sb("hT", [P, C, SEQ])
        work = sb("work", [P, 5632])
        cst = sb("cst", [P, CONST_COLS])
        gains = sb("gains", [P, 2 * LAYERS, C])
        w_rt = sb("w_rt", [P, LAYERS, C, GROUPS + EXPERTS])
        b_rt = sb("b_rt", [P, LAYERS, GROUPS + EXPERTS])
        small = sb("small", [P, 320])
        idx_u = sb("idx_u", [P, 2 * T, 8], U32)
        rounds_i = sb("rounds_i", [P, LAYERS], I32)
        psum = [ctx.enter_context(nc.psum_tensor(f"bank{i}", [P, 512], F32)) for i in range(8)]

        def const(name, *shape):
            at, w = CONST_AT[name]
            v = cst[:, at:at + w]
            if len(shape) == 2:
                v = v.rearrange("p (a b) -> p a b", a=shape[0])
            return v

        ident = const("ident")
        xn_t = xn[:, :].rearrange("p (t d) -> p t d", t=T)
        h_c = h[:, :, :].rearrange("p t (q c) -> p t c q", c=C)
        xn_c = xn[:, :].rearrange("p (t c q) -> p t c q", t=T, c=C)
        rot = [xn[:, 512 * i:512 * i + 512] for i in range(3)]
        rot_tmp = xn[:, 1536:2048]
        oT = hT
        h_low = sb_at("h_low", [P, C, SEQ], hT_at, F32R)
        h_high = sb_at("h_high", [P, C, SEQ], ring_at + 4 * (8 * UNIT + 2048), F32R)
        split = sb_at("split", [P, PARTS, 2, 512], ring_at + 4 * 6 * UNIT, F32R)
        w_high = [split[:, b, 0, :] for b in range(PARTS)]
        w_low = [split[:, b, 1, :] for b in range(PARTS)]
        qT = ring[:, 8, 0:2048].rearrange("p (a s) -> p a s", a=8)
        kT = ring[:, 7, :].rearrange("p (h s) -> p h s", h=16)
        probT = [xn[:, 384 * i:384 * i + 384] for i in range(4)]
        v_sb = work[:, 0:2048].rearrange("p (t d) -> p t d", t=T)
        rg = work[:, 2048:3072].rearrange("p (t d) -> p t d", t=T)
        prob = [work[:, 3072 + 384 * i:3072 + 384 * i + 384] for i in range(4)]
        o_ret = work[:, 4608:5632].rearrange("p (t d) -> p t d", t=T)
        onehot = work[:, 0:192].rearrange("p (t k s) -> p t k s", t=T, k=GE)
        gated = work[:, 192:384].rearrange("p (t k s) -> p t k s", t=T, k=GE)
        gated_twice = work[:, 5120:5376].rearrange("p (t b k s) -> p t b k s", t=T, b=2, k=TAIL)
        gatedT = work[:, 384:640]
        xT = work[:, 640:1408].rearrange("p (c s) -> p c s", c=C)
        eg = [work[:, 1408 + 128 * i:1536 + 128 * i] for i in range(2)]
        gu = [work[:, 1664 + 256 * i:1920 + 256 * i] for i in range(2)]
        hid = [work[:, 2176 + 128 * i:2304 + 128 * i] for i in range(2)]
        hidT = [work[:, 2432 + 128 * i:2560 + 128 * i] for i in range(GE)]
        y_sb = work[:, 2816:3840]
        masked = work[:, 3840:3904].rearrange("p (t e) -> p t e", t=T)
        chosen = work[:, 3904:4032].rearrange("p (t c e) -> p t c e", t=T, c=2)
        lf = work[:, 4032:4096].rearrange("p (t e) -> p t e", t=T)
        gain_row = work[:, 4096:5120]
        sumsq, var, rstd, newt = (small[:, 2 * i:2 * i + 2] for i in range(4))
        den = small[:, 8:40].rearrange("p (h t) -> p h t", t=T)
        rden = small[:, 40:88].rearrange("p (h b) -> p h b", b=3)
        neg_rstd = small[:, 92:94]
        negm = small[:, 104:136].rearrange("p (h t) -> p h t", t=T)
        sq = small[:, 88:92].rearrange("p (t a) -> p t a", t=T)
        lg = small[:, 136:152].rearrange("p (t e) -> p t e", t=T)
        top = small[:, 152:184].rearrange("p (a e) -> p a e", a=2 * T)
        idx = small[:, 184:190]
        gv = small[:, 192:208]
        pen = small[:, 208:216].rearrange("p (t e) -> p t e", t=T)
        rstat = small[:, 224:240].rearrange("p (t h m) -> p t h m", t=T, h=RET)
        rvar = small[:, 240:248]
        rrstd = small[:, 248:256]
        bnst = small[:, 258:306].rearrange("p (a s) -> p a s", a=2 * RET)
        expg = small[:, 306:314].rearrange("p (t e) -> p t e", t=T)
        half_exp = small[:, 314:316]
        cnt = small[:, 316:318]
        posm = sb("posm", [P, T, 36])
        gate = sb("gate", [P, T, 36])
        asg = sb("asg", [P, T, EXPERTS])
        gterm = sb("gterm", [P, T, 2, EXPERTS])
        limhit = sb("limhit", [P, MAX_ROUNDS - 1])

        x_loaded = sems("x_loaded", T)
        w_begun = sem("w_begun")
        const_loaded = sems("const_loaded", 2)
        gain_loaded = sems("gain_loaded", 2 * LAYERS)
        router_loaded = sem("router_loaded")
        w_arrived = sems("w_arrived", 8)
        e_arrived = [sems(f"e_arrived{l}_", 9) for l in range(LAYERS)]
        fin_loaded = sem("fin_loaded")
        out_stored = sem("out_stored")
        squared = sem("squared")
        var_ready = sem("var_ready")
        pow_ready = sem("pow_ready")
        rstd_ready = sem("rstd_ready")
        xn_ready = sem("xn_ready")
        h_turned = sem("h_turned")
        hT_ready = sem("hT_ready")
        h_high_ready = sem("h_high_ready")
        w_high_ready = sem("w_high_ready")
        w_low_ready = sem("w_low_ready")
        chunk_used = sem("chunk_used")
        dve_norm = sem("dve_norm")
        warm_ready = sem("warm_ready")
        proj_done = sems("proj_done", LAYERS)
        bank_out = [sems(f"bank_out{l}_", 4) for l in range(LAYERS)]
        rot_ready = sems("rot_ready", LAYERS)
        rot_turned = sems("rot_turned", LAYERS)
        qkT_ready = sems("qkT_ready", LAYERS)
        k_cleared = sems("k_cleared", LAYERS)
        s_done = sems("s_done", LAYERS)
        s_out = sems("s_out", LAYERS)
        exp_done = sems("exp_done", LAYERS)
        den_ready = sems("den_ready", LAYERS)
        p_ready = sems("p_ready", LAYERS)
        p_turned = sems("p_turned", LAYERS)
        pT_ready = sems("pT_ready", LAYERS)
        pair_done = sems("pair_done", LAYERS)
        oT_ready = sems("oT_ready", LAYERS)
        ret_ready = sem("ret_ready")
        ret_done = sem("ret_done")
        ret_var = sem("ret_var")
        ret_pow = sem("ret_pow")
        ret_normed = sem("ret_normed")
        ret_turned = sem("ret_turned")
        retT_ready = sem("retT_ready")
        mixed = sems("mixed", LAYERS)
        mix_added = sems("mix_added", LAYERS)
        dve_attn = sems("dve_attn", LAYERS)
        logits_done = sems("logits_done", LAYERS)
        gmax_ready = sems("gmax_ready", LAYERS)
        gexp_done = sems("gexp_done", LAYERS)
        assigned = sems("assigned", LAYERS)
        counts_done = sems("counts_done", LAYERS)
        pos_done = sems("pos_done", LAYERS)
        first_gates = sem("first_gates")
        gate_steps = sems("gate_steps", LAYERS)
        rounds_ready = sems("rounds_ready", LAYERS)
        dve_route = sems("dve_route", LAYERS)
        onehot_ready = sems("onehot_ready", LAYERS)
        gated_ready = sems("gated_ready", LAYERS)
        gated_turned = sems("gated_turned", LAYERS)
        gatedT_ready = sems("gatedT_ready", LAYERS)
        gathered = sems("gathered", LAYERS)
        xT_ready = sems("xT_ready", LAYERS)
        gate_up_done = sems("gate_up_done", LAYERS)
        gate_up_out = sems("gate_up_out", LAYERS)
        hid_ready = sems("hid_ready", LAYERS)
        hid_turned = sems("hid_turned", LAYERS)
        hidT_ready = sems("hidT_ready", LAYERS)
        down_done = sems("down_done", LAYERS)
        y_low = sems("y_low", LAYERS)
        y_high = sems("y_high", LAYERS)
        scattered = sems("scattered", LAYERS)
        added = sems("added", LAYERS)
        dve_moe = sems("dve_moe", LAYERS)

        n_ret = [RET, 0]
        n_items = [n_ret[l] + HEADS[l] for l in range(LAYERS)]
        n_rot = [ROTATED[l] * T for l in range(LAYERS)]

        def mix_bank(n, t):
            return psum[t if n == 0 else 6 + t]

        block = ctx.enter_context(nc.Block())

        @block.sync
        def _(sp):
            gate_rows = w_gate.rearrange("l e (p c) n -> (l e) p (c n)", c=C)
            up_rows = w_up.rearrange("l e (p c) n -> (l e) p (c n)", c=C)
            down_rows = w_down.rearrange("l e (j p) n -> (l e) p j n", p=P)

            def load_group(l, r, g, experts, first_expert, after_attention=False):
                for k in range(experts):
                    if after_attention:
                        sp.wait_ge(proj_done[l], 2 * T * (k + 1))
                    else:
                        sp.wait_ge(gate_up_done[l], gu_count(r, g, k) - GE)
                    if after_attention and k == experts - 1:
                        load_w_out(l, 0)
                    row = l * EXPERTS + first_expert + k
                    sp.dma_start(ring[:, 2 * k, :], gate_rows[row]).then_inc(e_arrived[l][2 * k], 16)
                    sp.dma_start(ring[:, 2 * k + 1, :], up_rows[row]).then_inc(e_arrived[l][2 * k + 1], 16)
                def load_down(k):
                    row = l * EXPERTS + first_expert + k
                    sp.dma_start(ring[:, 6 + k, :].rearrange("p (j n) -> p j n", j=HID // P),
                                 down_rows[row]).then_inc(e_arrived[l][6 + k], 16)

                if after_attention:
                    sp.wait_ge(s_done[l], n_items[l])
                    load_w_out(l, 1)
                    load_down(2)
                    for k in range(2):
                        sp.wait_ge(mixed[l], T * (k + 1))
                        load_down(k)
                else:
                    sp.wait_ge(down_done[l], down_no(r, g))
                    for k in range(experts):
                        if experts == GE or k < experts - 1:
                            load_down(k)
                        else:
                            row = l * EXPERTS + first_expert + k
                            slot = ring[:, 6 + k, :].rearrange("p (j n) -> p j n", j=HID // P)
                            for half, arrived in ((0, e_arrived[l][6 + k]), (1, e_arrived[l][7 + k])):
                                cols = slice(512 * half, 512 * half + 512)
                                sp.dma_start(slot[:, :, cols], down_rows[row][:, :, cols]).then_inc(arrived, 16)

            def load_w_out(l, n):
                sp.dma_start(ring[:, 6 + n, :].rearrange("p (c n) -> p c n", c=C),
                             w_out[l][0].rearrange("(c p) n -> p c n", p=P)[:, :, 512 * n:512 * n + 512])\
                  .then_inc(w_arrived[6 + n], 16)

            def load_round(l, r, after_attention=False):
                if after_attention:
                    load_group(l, r, 0, GE, 0, after_attention)
                with sp.Fori(int(after_attention), FULL) as g:
                    load_group(l, r, g, GE, g * GE)
                load_group(l, r, FULL, TAIL, FULL * GE)

            for t in range(T):
                sp.dma_start(h[:, t, :], x[0, P * t:P * t + P, :]).then_inc(x_loaded[t], 16)
            sp.dma_start(cst[:, 0:FIRST_CONSTS], consts[:, 0:FIRST_CONSTS]).then_inc(const_loaded[0], 16)

            def load_gain(i, g):
                sp.dma_start(gains[:, i, :], g.rearrange("(p c) -> p c", c=C)).then_inc(gain_loaded[i], 16)

            load_gain(0, mix[0][0])
            more = None
            for l in range(LAYERS):
                w_in_v = w_in[l][0].rearrange("(p c) n -> p c n", c=C)
                for j in range(NW):
                    if l:
                        sp.wait_ge(gate_up_done[l - 1],
                                   gu_count(more, FULL, j // 2))
                    b = BLOCKS[l][j]
                    block, source = ring[:, j, :].rearrange("p (c n) -> p c n", c=C), w_in_v[:, :, 512 * b:512 * b + 512]
                    if j == 0:
                        sp.dma_start(block[:, 0:C // 2, :], source[:, 0:C // 2, :]).then_inc(w_begun, 16)
                        sp.dma_start(block[:, C // 2:, :], source[:, C // 2:, :]).then_inc(w_arrived[j], 16)
                        if l == 0:
                            for i, g in ((1, ffn_norm[0]), (2, mix[1][0]), (3, ffn_norm[1])):
                                load_gain(i, g)
                    else:
                        sp.dma_start(block, source).then_inc(w_arrived[j], 16)
                    if l == 0 and j == 2:
                        sp.dma_start(cst[:, FIRST_CONSTS:], consts[:, FIRST_CONSTS:]).then_inc(const_loaded[1], 16)
                if l == 0:
                    for m in range(LAYERS):
                        for dst, src in ((w_rt[:, m, :, 0:GROUPS], w_group[m].rearrange("(p c) e -> p c e", c=C)),
                                         (w_rt[:, m, :, GROUPS:], w_fine[m].rearrange("(p c) e -> p c e", c=C)),
                                         (b_rt[:, m, 0:GROUPS], b_group[m].partition_broadcast(P)),
                                         (b_rt[:, m, GROUPS:], b_fine[m].partition_broadcast(P))):
                            sp.dma_start(dst, src).then_inc(router_loaded, 16)
                load_round(l, 0, after_attention=True)
                sp.wait_ge(rounds_ready[l], 1)
                more = sp.value_load(rounds_i[0:1, l:l + 1], min_val=0, max_val=MAX_ROUNDS - 1)
                with sp.If(more > 0):
                    with sp.Fori(1, more + 1) as r:
                        load_round(l, r)
            for t in range(T):
                sp.wait_ge(xn_ready, T * LAYERS + t + 1)
                sp.dma_start(out[0, P * t:P * t + P, :], xn_t[:, t, :]).then_inc(out_stored, 16)
            sp.wait_ge(out_stored, T * 16)

        @block.gpsimd
        def _(pool):
            pool.memset(half_exp, -0.5).then_inc(pow_ready, 1)
            pool.wait_ge(pow_ready, 1)

            def rsqrt_norm(ph):
                for t in range(T):
                    pool.wait_ge(var_ready, T * ph + t + 1)
                    pool.tensor_tensor(rstd[:, t:t + 1], var[:, t:t + 1], half_exp[:, 0:1], ALU.pow).then_inc(pow_ready, 1)

            def gates(l):
                steps = 0

                def step(ins):
                    nonlocal steps
                    steps += 1
                    ins.then_inc(gate_steps[l], 1)
                    pool.wait_ge(gate_steps[l], steps)

                e, by = gv[:, 4:6], gv[:, 8:10]
                weight = gv[:, 10:14].rearrange("p (t c) -> p t c", t=T)
                pool.wait_ge(first_gates, l + 1)
                step(pool.tensor_tensor(weight[:, :, 0], by, const("ones")[:, 0:T], ALU.mult))
                step(pool.tensor_tensor(weight[:, :, 1], by, e, ALU.mult))
                step(pool.tensor_tensor(gterm[:], chosen, weight.unsqueeze(3).broadcast_to([P, T, 2, EXPERTS]),
                                        ALU.mult))
                step(pool.tensor_tensor(gate[:, :, 0:EXPERTS], gterm[:, :, 0, :], gterm[:, :, 1, :], ALU.add))
                assert steps == GATE_STEPS

            for l in range(LAYERS):
                rsqrt_norm(2 * l)
                pairs = kT.rearrange("p (a b) s -> p a b s", b=2)
                pool.wait_ge(pow_ready, 1 + T * (2 * l + 1))
                pool.memset(pairs[HEAD:P, :, 0, :], 0.0).then_inc(k_cleared[l], 1)
                pool.wait_ge(k_cleared[l], 1)
                pool.memset(pairs[0:HEAD, :, 1, :], 0.0).then_inc(k_cleared[l], 1)
                pool.wait_ge(k_cleared[l], 2)
                for m in range(HEADS[l]):
                    if l == 0 and m == 3:
                        pool.wait_ge(ret_var, 1)
                        pool.tensor_tensor(rrstd, rvar, half_exp[:, 0:1].broadcast_to([P, 8]),
                                           ALU.pow).then_inc(ret_pow, 1)
                    pool.wait_ge(den_ready[l], m + 1)
                    b = prob[(n_ret[l] + m) % 4].rearrange("p (b s) -> p b s", b=3)
                    pool.tensor_tensor(b, b, rden[:, m, :].unsqueeze(2).broadcast_to([P, 3, P]), ALU.mult)\
                        .then_inc(p_ready[l], 1)
                rsqrt_norm(2 * l + 1)
                gates(l)
            rsqrt_norm(2 * LAYERS)

        @block.scalar
        def _(act):
            def square(ph, t, half):
                act.activation(xn_t[:, t, 512 * half:512 * half + 512], h[:, t, 512 * half:512 * half + 512],
                               ACT.Square, accum_out=sq[:, t, half:half + 1]).then_inc(squared, 1)

            for t in range(T):
                act.wait_ge(x_loaded[t], 16)
                for half in range(2):
                    square(0, t, half)

            def copy_qkT(l, s):
                act.wait_ge(rot_turned[l], s + 1)
                j, t = divmod(s, T)
                src = psum[4 + s % 2][:, :].rearrange("p (a s) -> p a s", a=4)
                cols = slice(P * t, P * t + P)
                if l == 0:
                    q_pairs, k_pairs = (((0, 4), None), (None, (0, 4)), ((4, 2), (4, 2)))[j]
                else:
                    q_pairs, k_pairs = (((0, 4), None), ((4, 4), None), (None, (0, 4)), (None, (4, 4)))[j]
                if q_pairs:
                    a, n = q_pairs
                    last = act.copy(qT[:, a:a + n, cols], src[:, 0:n, :])
                if k_pairs:
                    a, n = k_pairs
                    if t == 0:
                        act.wait_ge(k_cleared[l], 2)
                    kv = kT.rearrange("p (a b) s -> p a b s", b=2)
                    act.copy(kv[0:HEAD, a:a + n, 0, cols], src[0:HEAD, 4 - n:4, :])
                    last = act.copy(kv[HEAD:P, a:a + n, 1, cols], src[HEAD:P, 4 - n:4, :])
                last.then_inc(qkT_ready[l], 1)

            def exponentials(l, m):
                act.wait_ge(s_out[l], m + 1)
                b = prob[(n_ret[l] + m) % 4]
                for t, cols in ((0, slice(0, P)), (1, slice(P, 3 * P))):
                    sums = {"accum_out": den[:, m, t:t + 1]} if l == 0 else {}
                    last = act.activation(b[:, cols], b[:, cols], ACT.Exp, bias=negm[:, m, t:t + 1], scale=-1.0, **sums)
                last.then_inc(exp_done[l], 1)

            def copy_pT(l, m):
                act.wait_ge(p_turned[l], m + 1)
                if m >= 4:
                    act.wait_ge(pair_done[l], (m - 4) // 2 + 1)
                act.copy(probT[m % 4], psum[2 + m % 2][:, 0:3 * P]).then_inc(pT_ready[l], 1)

            def copy_oT(l, a):
                act.wait_ge(pair_done[l], a + 1)
                act.copy(oT[:, a, :], psum[4 + a % 2][:, 0:SEQ]).then_inc(oT_ready[l], 1)

            def experts_of(l, r, g, n):
                no = group_no(r, g)
                act.wait_ge(gated_turned[l], no + 1)
                rows = y_rows(n)
                act.copy(gatedT[0:rows, :], psum[5][0:rows, 0:SEQ]).then_inc(gatedT_ready[l], 1)

                def copy_hidT(k):
                    act.wait_ge(hid_turned[l], expert_no(r, g, k) + 1)
                    act.copy(hidT[k], psum[4][:, 0:P]).then_inc(hidT_ready[l], 1)

                for k in range(n):
                    act.wait_ge(gate_up_done[l], gu_count(r, g, k))
                    if k >= 2:
                        act.wait_ge(hid_ready[l], expert_no(r, g, k) - 1)
                    bank = psum[2 + k % 2]
                    act.activation(eg[k % 2], bank[:, 0:P], ACT.Exp, scale=-1.0)
                    act.copy(gu[k % 2], bank[:, 0:2 * P]).then_inc(gate_up_out[l], 1)
                    if k:
                        copy_hidT(k - 1)
                copy_hidT(n - 1)
                act.wait_ge(down_done[l], down_no(r, g) + 1)
                act.copy(y_sb[0:rows, 0:512], psum[6][0:rows, :]).then_inc(y_low[l], 1)

            def split_hT(t):
                for q in range(2):
                    act.wait_ge(h_turned, 4 * (2 * l) + 2 * t + q + 1)
                    act.copy(h_high[:, 4 * q:4 * q + 4, P * t:P * t + P],
                             psum[2 * (1 - t) + q][:, :].rearrange("p (a s) -> p a s", a=4)).then_inc(h_high_ready, 1)

            def split_chunks(l, j, first_c, last_c):
                for c in range(first_c, last_c):
                    u = C * j + c
                    if j == 0 and c == 0:
                        act.wait_ge(w_begun, 16 * (l + 1))
                    elif c in (0, C // 2):
                        act.wait_ge(w_arrived[j], 16 * (l + 1))
                    if u >= PARTS:
                        before_j, before_c = divmod(u - PARTS, C)
                        if before_c == C - 1:
                            act.wait_ge(proj_done[l], T * (before_j + 1))
                        else:
                            act.wait_ge(chunk_used, (l * NW + before_j) * (C - 1) + before_c + 1)
                    act.activation(w_high[u % PARTS], ring[:, j, 512 * c:512 * c + 512], ACT.Copy,
                                   scale=gains[:, 2 * l, c:c + 1]).then_inc(w_high_ready, 1)

            def block_out(l, j):
                for t in range(T):
                    s = T * j + t
                    act.wait_ge(proj_done[l], s + 1)
                    act.wait_ge(rstd_ready, T * 2 * l + t + 1)
                    if l == 0 and j == RG:
                        act.activation(rg[:, t, :], psum[s % 4][:, :], ACT.Exp, scale=neg_rstd[:, t:t + 1])
                        act.activation(o_ret[:, t, :], psum[s % 4][:, :], ACT.Copy,
                                       scale=rstd[:, t:t + 1]).then_inc(bank_out[l][s % 4], 1)
                    else:
                        at = 512 * (j - (NW - 2))
                        act.activation(v_sb[:, t, at:at + 512], psum[s % 4][:, :], ACT.Copy,
                                       scale=rstd[:, t:t + 1]).then_inc(bank_out[l][s % 4], 1)

            for l in range(LAYERS):
                if l == 0:
                    for t in range(T):
                        split_hT(t)
                act.wait_ge(gain_loaded[2 * l], 16)
                for j in range(NW + 1):
                    parts = lambda a, b: split_chunks(l, j, a, b) if j < NW else None
                    parts(0, 4)
                    if l and j == 0:
                        for t in range(T):
                            split_hT(t)
                        for q in range(4):
                            act.wait_ge(added[l - 1], group_no(more, FULL) * 4 + (q + 1))
                            square(2 * l, q % 2, q // 2)
                    if j > ROTATED[l]:
                        block_out(l, j - 1)
                    parts(4, COPY_AT[0])
                    if 0 < j <= ROTATED[l]:
                        copy_qkT(l, T * (j - 1))
                    parts(COPY_AT[0], COPY_AT[1])
                    if 0 < j <= ROTATED[l]:
                        copy_qkT(l, T * (j - 1) + 1)
                    parts(COPY_AT[1], C)
                for i in range(HEADS[l] + LAG + 4):
                    if i < HEADS[l]:
                        exponentials(l, i)
                    if 0 <= i - LAG < HEADS[l]:
                        copy_pT(l, i - LAG)
                    if 0 <= i - LAG - 3 < HEADS[l] and (i - LAG) % 2 == 0:
                        copy_oT(l, (i - LAG - 3) // 2)
                    if l == 0 and i == HEADS[l] + 2:
                        for t in range(T):
                            act.wait_ge(ret_turned, t + 1)
                            act.copy(oT[:, 4:8, P * t:P * t + P],
                                     psum[6 + t][:, :].rearrange("p (a s) -> p a s", a=4)).then_inc(retT_ready, 1)
                for n in range(2):
                    for t in range(T):
                        act.wait_ge(mix_added[l], 2 * n + t + 1)
                        square(2 * l + 1, t, n)
                for t in range(T):
                    act.wait_ge(gmax_ready[l], t + 1)
                    act.activation(expg[:, t, :], lg[:, t, 0:GROUPS], ACT.Exp, bias=gv[:, t:t + 1],
                                   accum_out=gv[:, 2 + t:3 + t])
                    act.activation(gv[:, 4 + t:5 + t], gv[:, 6 + t:7 + t], ACT.Exp).then_inc(gexp_done[l], 1)
                if l == LAYERS - 1:
                    act.dma_start(gain_row, final_norm.partition_broadcast(P)).then_inc(fin_loaded, 16)

                def full_groups(r):
                    with act.Fori(0, FULL) as g:
                        experts_of(l, r, g, GE)

                full_groups(0)
                act.wait_ge(rounds_ready[l], 1)
                more = act.value_load(rounds_i[0:1, l:l + 1], min_val=0, max_val=MAX_ROUNDS - 1)
                experts_of(l, 0, FULL, TAIL)
                with act.If(more > 0):
                    with act.Fori(1, more + 1) as r:
                        full_groups(r)
                        experts_of(l, r, FULL, TAIL)
                if l == LAYERS - 1:
                    for q in range(4):
                        act.wait_ge(added[l], group_no(more, FULL) * 4 + (q + 1))
                        square(2 * l + 2, q % 2, q // 2)

        @block.tensor
        def _(pe):
            def keep_warm(n, data):
                for _ in range(n):
                    pe.matmul(psum[7][:, :], data[:, 0:P], data, start=True, stop=True)

            def turn_h(t):
                for q in range(2):
                    for c in range(4):
                        last = pe.transpose(psum[2 * (1 - t) + q][:, P * c:P * c + P], h_c[:, t, 4 * q + c, :], ident)
                    last.then_inc(h_turned, 1)

            def project(l, j, first_c, last_c):
                for c in range(first_c, last_c):
                    u = C * j + c
                    if u == 0:
                        pe.wait_ge(hT_ready, 4 * (2 * l) + 4)
                    pe.wait_ge(w_low_ready, l * NW * C + u + 1)
                    for t in range(T):
                        s = T * j + t
                        if c == 0 and j >= 2:
                            pe.wait_ge(bank_out[l][s % 4], s // 4)
                        high, low = h_high[:, c, P * t:P * t + P], h_low[:, c, P * t:P * t + P]
                        wh, wl = w_high[u % PARTS], w_low[u % PARTS]
                        bank = psum[s % 4][:, :]
                        pe.matmul(bank, high, wh, start=(c == 0), stop=False)
                        pe.matmul(bank, low, wh, start=False, stop=False)
                        last = pe.matmul(bank, high, wl, start=False, stop=(c == C - 1))
                        if c == C - 1:
                            last.then_inc(proj_done[l], 1)
                    if c < C - 1:
                        last.then_inc(chunk_used, 1)

            def turn_rot(l, s):
                pe.wait_ge(rot_ready[l], s + 1)
                if s >= 2:
                    pe.wait_ge(qkT_ready[l], s - 1)
                for a in range(4):
                    last = pe.transpose(psum[4 + s % 2][:, P * a:P * a + P], rot[s % 3][:, P * a:P * a + P], ident)
                last.then_inc(rot_turned[l], 1)

            def scores(l, i):
                before = i - 2
                if 0 <= before < n_ret[l]:
                    pe.wait_ge(ret_ready, before + 1)
                elif before >= 0:
                    pe.wait_ge(s_out[l], before - n_ret[l] + 1)
                bank = psum[i % 2]
                if i < n_ret[l]:
                    q, k = qT[:, 4 + i // 2, :], kT[:, HEADS[l] + i, :]
                    pe.matmul(bank[:, 0:2 * P], k[:, 0:P], q, start=True, stop=True)
                    last = pe.matmul(bank[:, 2 * P:3 * P], k[:, P:SEQ], q[:, P:SEQ], start=True, stop=True)
                else:
                    m = i - n_ret[l]
                    q, k = qT[:, m // 2, :], kT[:, m, :]
                    pe.matmul(bank[:, 0:P], q[:, 0:P], k[:, 0:P], start=True, stop=True)
                    last = pe.matmul(bank[:, P:3 * P], q[:, P:SEQ], k, start=True, stop=True)
                last.then_inc(s_done[l], 1)

            def retain(n):
                pe.wait_ge(ret_ready, n + 1)
                w = prob[n]
                for t, b, kt in ((0, 0, 0), (1, 1, 0), (1, 2, 1)):
                    last = pe.matmul(psum[6 + t][:, P * n:P * n + P], w[:, P * b:P * b + P],
                                     v_sb[:, kt, 512 + P * n:512 + P * n + P], start=(kt == 0), stop=(t == kt))
                last.then_inc(ret_done, 1)

            def turn_p(l, m):
                pe.wait_ge(p_ready[l], m + 1)
                if m >= 2:
                    pe.wait_ge(pT_ready[l], m - 1)
                b4 = prob[(n_ret[l] + m) % 4]
                for b in range(3):
                    last = pe.transpose(psum[2 + m % 2][:, P * b:P * b + P], b4[:, P * b:P * b + P], ident)
                last.then_inc(p_turned[l], 1)

            def values(l, a):
                pe.wait_ge(pT_ready[l], 2 * a + 2)
                if a >= 2:
                    pe.wait_ge(oT_ready[l], a - 1)
                bank = psum[4 + a % 2]
                for kt in range(T):
                    for m in (2 * a, 2 * a + 1):
                        lo = HEAD * (m % 2)
                        cols = slice(P * kt, SEQ)
                        pT = probT[m % 4][:, 0:SEQ] if kt == 0 else probT[m % 4][:, SEQ:SEQ + P]
                        last = pe.matmul(bank[lo:lo + HEAD, cols], v_sb[:, kt, HEAD * m:HEAD * m + HEAD], pT,
                                         start=(kt == 0), stop=(kt == T - 1), tile_position=(0, lo))
                last.then_inc(pair_done[l], 1)

            def experts_of(l, r, g, n):
                no = group_no(r, g)
                rows = SLOTS * n
                pe.wait_ge(onehot_ready[l], no + 1)
                for c in range(C):
                    for t in range(T):
                        last = pe.matmul(psum[c // 4][:, rows * (c % 4):rows * (c % 4) + rows],
                                         xn_c[:, t, c, :], onehot[:, t, 0:n, :].rearrange("p k s -> p (k s)"),
                                         start=(t == 0), stop=(t == T - 1))
                    if c % 4 == 3:
                        last.then_inc(gathered[l], 1)
                pe.wait_ge(gated_ready[l], no + 1)
                for t in range(T):
                    weights = gated[:, t, :, :].rearrange("p k s -> p (k s)") if n == GE else \
                        gated_twice[:, t, :, :, :].rearrange("p b k s -> p (b k s)")
                    last = pe.transpose(psum[5][0:y_rows(n), P * t:P * t + P], weights, ident)
                last.then_inc(gated_turned[l], 1)
                pe.wait_ge(xT_ready[l], no * 2 + 1)

                def turn_hid(k):
                    e = expert_no(r, g, k)
                    pe.wait_ge(hid_ready[l], e + 1)
                    if k:
                        pe.wait_ge(hidT_ready[l], e)
                    pe.transpose(psum[4][:, 0:P], hid[k % 2], ident).then_inc(hid_turned[l], 1)

                for k in range(n):
                    e = expert_no(r, g, k)
                    if k >= 2:
                        pe.wait_ge(gate_up_out[l], e - 1)
                    pe.wait_ge(e_arrived[l][2 * k], arrivals(2 * k, r, g))
                    pe.wait_ge(e_arrived[l][2 * k + 1], arrivals(2 * k + 1, r, g))
                    bank = psum[2 + k % 2]
                    for c in range(C):
                        if k == 0 and c == C // 2:
                            pe.wait_ge(xT_ready[l], no * 2 + 2)
                        for j in range(4):
                            last = pe.matmul(
                                bank[32 * j:32 * j + 32, 0:2 * P].rearrange("p (a s) -> p a s", a=2),
                                xT[:, c, SLOTS * k:SLOTS * k + SLOTS],
                                ring[:, 2 * k:2 * k + 2, 512 * c + P * j:512 * c + P * j + P],
                                start=(c == 0), stop=(c == C - 1), tile_position=(0, 32 * j))
                    last.then_inc(gate_up_done[l], 1 if n == GE or k < n - 1 else 1 + GE - n)
                    if k:
                        turn_hid(k - 1)
                turn_hid(n - 1)
                if n == GE:
                    for k in range(n):
                        if k == n - 1:
                            keep_warm(6, cst[:, 0:512])
                        pe.wait_ge(e_arrived[l][6 + k], arrivals(6 + k, r, g))
                    pe.wait_ge(hidT_ready[l], expert_no(r, g, n))
                    for j in range(HID // P):
                        for half in range(2):
                            for k in range(n):
                                last = pe.matmul(
                                    psum[6 + half][32 * k:32 * k + 32, :], hidT[k][:, 32 * j:32 * j + 32],
                                    ring[:, 6 + k, D * j + 512 * half:D * j + 512 * half + 512],
                                    start=(j == 0), stop=(j == HID // P - 1), tile_position=(0, 32 * k))
                    last.then_inc(down_done[l], 1)
                else:
                    def down(k, half):
                        for jj in range(2):
                            for b in range(2):
                                j, at = 2 * b + jj, 32 * (2 * b + k)
                                last = pe.matmul(
                                    psum[6 + half][at:at + 32, :], hidT[k][:, 32 * j:32 * j + 32],
                                    ring[:, 6 + k, D * j + 512 * half:D * j + 512 * half + 512],
                                    start=(jj == 0), stop=(jj == 1), tile_position=(0, at))
                        if k == n - 1:
                            last.then_inc(down_done[l], 1)

                    for k in range(n):
                        pe.wait_ge(hidT_ready[l], expert_no(r, g, k) + 1)
                        for half, at in ((0, 6 + k), (1, 6 + k if k < n - 1 else 7 + k)):
                            pe.wait_ge(e_arrived[l][at], arrivals(at, r, g))
                            down(k, half)
                pe.wait_ge(gatedT_ready[l], no + 1)
                for q in range(4):
                    half, t = divmod(q, 2)
                    if t == 0:
                        pe.wait_ge((y_low, y_high)[half][l], no + 1)
                    if q >= 2:
                        pe.wait_ge(added[l], no * 4 + (q - 1))
                    pe.matmul(psum[q % 2][:, :], gatedT[0:y_rows(n), P * t:P * t + P],
                              y_sb[0:y_rows(n), 512 * half:512 * half + 512], start=True, stop=True)\
                      .then_inc(scattered[l], 1)

            def mix_product(l, n, t, features=range(C)):
                for c in features:
                    last = pe.matmul(mix_bank(n, t)[:, :], oT[:, c, P * t:P * t + P],
                                     ring[:, 6 + n, 512 * c:512 * c + 512],
                                     start=(c == MIX_ORDER[l][0]), stop=(c == MIX_ORDER[l][-1]))
                if c == MIX_ORDER[l][-1]:
                    last.then_inc(mixed[l], 1)

            def mix_early(l, features):
                pe.wait_ge(w_arrived[6], 16 * (l + 1))
                for c in features:
                    if c < HEADS[l] // 2:
                        pe.wait_ge(oT_ready[l], c + 1)
                    else:
                        pe.wait_ge(retT_ready, T)
                    for t in range(T):
                        mix_product(l, 0, t, (c,))

            def turn_retained():
                for t in range(T):
                    pe.wait_ge(ret_normed, t + 1)
                    for c in range(4):
                        last = pe.transpose(psum[6 + t][:, P * c:P * c + P], o_ret[:, t, P * c:P * c + P], ident)
                    last.then_inc(ret_turned, 1)

            def turn_mixed(l, t):
                pe.wait_ge(mix_added[l], T + t + 1)
                turn_h(t)

            def logits(l, t):
                pe.wait_ge(hT_ready, 4 * (2 * l + 1) + 2 * t + 2)
                for c in range(C):
                    last = pe.matmul(psum[4 + t][:, 0:36], hT[:, c, P * t:P * t + P],
                                     w_rt[:, l, c, :], start=(c == 0), stop=(c == C - 1))
                last.then_inc(logits_done[l], 1)

            pe.wait_ge(warm_ready, 1)
            keep_warm(3, work[:, 0:512])
            pe.wait_ge(const_loaded[0], 16)
            for t in range(T):
                pe.wait_ge(x_loaded[t], 16)
                turn_h(t)
            for l in range(LAYERS):
                if l == 0:
                    keep_warm(1, work[:, 0:512])
                for j in range(NW):
                    turns = 0 < j <= ROTATED[l]
                    project(l, j, 0, TURN_AT[0])
                    if turns:
                        turn_rot(l, T * (j - 1))
                    project(l, j, TURN_AT[0], TURN_AT[1])
                    if turns:
                        turn_rot(l, T * (j - 1) + 1)
                    project(l, j, TURN_AT[1], C)
                pe.wait_ge(qkT_ready[l], n_rot[l])
                for b in range(2):
                    pe.wait_ge(bank_out[l][b], 3)
                for i in range(n_items[l] + LAG + 3):
                    m = i - n_ret[l]
                    if i < n_items[l]:
                        scores(l, i)
                    if i == 2:
                        for b in range(2, 4):
                            pe.wait_ge(bank_out[l][b], 3)
                    if 0 <= i - 2 < n_ret[l]:
                        retain(i - 2)
                    if 0 <= m - LAG < HEADS[l]:
                        turn_p(l, m - LAG)
                    if 0 <= m - LAG - 2 < HEADS[l] and (m - LAG) % 2:
                        values(l, (m - LAG - 2) // 2)
                    if l == 0 and m == HEADS[l] + 2:
                        turn_retained()
                    if m - HEADS[l] in MIX_EARLY[l]:
                        if m == HEADS[l] + 1:
                            pe.wait_ge(s_out[l], HEADS[l])
                        mix_early(l, MIX_EARLY[l][m - HEADS[l]])
                early = sum(MIX_EARLY[l].values(), ())
                mix_early(l, MIX_ORDER[l][len(early):])
                order = MIX_ORDER[l]
                pe.wait_ge(w_arrived[7], 16 * (l + 1))
                mix_product(l, 1, 0, order)
                mix_product(l, 1, 1, order[:2])
                turn_mixed(l, 0)
                mix_product(l, 1, 1, order[2:LOGITS_AT])
                pe.wait_ge(router_loaded, 8 * 16)
                logits(l, 0)
                mix_product(l, 1, 1, order[LOGITS_AT:])
                turn_mixed(l, 1)
                logits(l, 1)
                before, ones = const("before"), const("ones")
                pe.wait_ge(assigned[l], 1)
                pe.matmul(psum[6][:, 0:32], before, asg[:, 0, :], start=True, stop=True)
                pe.matmul(psum[6][:, 32:64], ones, asg[:, 0, :], start=True, stop=False)
                pe.matmul(psum[4][:, 0:32], ones, asg[:, 0, :], start=True, stop=False)
                keep_warm(2, cst[:, 0:512])
                pe.wait_ge(assigned[l], 2)
                pe.matmul(psum[4][:, 0:32], ones, asg[:, 1, :], start=False, stop=True).then_inc(counts_done[l], 1)
                pe.matmul(psum[6][:, 32:64], before, asg[:, 1, :], start=False, stop=True).then_inc(pos_done[l], 1)
                keep_warm(1, cst[:, 0:512])
                pe.wait_ge(xn_ready, T * l + T)

                def full_groups(r):
                    with pe.Fori(0, FULL) as g:
                        experts_of(l, r, g, GE)

                full_groups(0)
                pe.wait_ge(rounds_ready[l], 1)
                more = pe.value_load(rounds_i[0:1, l:l + 1], min_val=0, max_val=MAX_ROUNDS - 1)
                experts_of(l, 0, FULL, TAIL)
                with pe.If(more > 0):
                    with pe.Fori(1, more + 1) as r:
                        full_groups(r)
                        experts_of(l, r, FULL, TAIL)
                if l < LAYERS - 1:
                    for t in range(T):
                        pe.wait_ge(added[l], group_no(more, FULL) * 4 + (3 + t))
                        turn_h(t)

        @block.vector
        def _(dve):
            norm_link = Chain(dve, dve_norm).link

            def variance(ph, t, squares):
                one = slice(t, t + 1)
                dve.wait_ge(squared, 4 * ph + squares)
                norm_link(dve.tensor_tensor(sumsq[:, one], sq[:, t, 0:1], sq[:, t, 1:2], ALU.add))
                dve.tensor_scalar(var[:, one], sumsq[:, one], 1.0 / D, EPS, ALU.mult, ALU.add).then_inc(var_ready, 1)

            def inverse_root(ph, t):
                one, link = slice(t, t + 1), norm_link
                dve.wait_ge(pow_ready, T * ph + t + 2)
                link(dve.scalar_tensor_tensor(out=newt[:, one], in0=rstd[:, one], scalar=var[:, one],
                                              in1=rstd[:, one], op0=ALU.mult, op1=ALU.mult))
                link(dve.tensor_scalar(newt[:, one], newt[:, one], -0.5, 1.5, ALU.mult, ALU.add))
                if ph == 0:
                    link(dve.scalar_tensor_tensor(out=neg_rstd[:, one], in0=rstd[:, one], scalar=-1.0,
                                                  in1=newt[:, one], op0=ALU.mult, op1=ALU.mult))
                dve.tensor_tensor(rstd[:, one], rstd[:, one], newt[:, one], ALU.mult).then_inc(rstd_ready, 1)
                dve.wait_ge(rstd_ready, T * ph + t + 1)

            def scale_rows(t):
                dve.tensor_scalar(xn_c[:, t, :, :], h[:, t, :].rearrange("p (q c) -> p c q", c=C),
                                  rstd[:, t:t + 1], None, ALU.mult).then_inc(xn_ready, 1)

            def split_columns(ph, t):
                for q in range(2):
                    dve.wait_ge(h_high_ready, 4 * (ph // 2) + 2 * t + q + 1)
                    part = (slice(None), slice(4 * q, 4 * q + 4), slice(P * t, P * t + P))
                    dve.tensor_tensor(h_low[part], psum[2 * (1 - t) + q][:, :].rearrange("p (a s) -> p a s", a=4),
                                      h_high[part], ALU.subtract).then_inc(hT_ready, 1)

            def split_chunks(l, j, first_c, last_c):
                for c in range(first_c, last_c):
                    u = C * j + c
                    dve.wait_ge(w_high_ready, l * NW * C + u + 1)
                    dve.scalar_tensor_tensor(out=w_low[u % PARTS], in0=ring[:, j, 512 * c:512 * c + 512],
                                             scalar=gains[:, 2 * l, c:c + 1], in1=w_high[u % PARTS],
                                             op0=ALU.mult, op1=ALU.subtract).then_inc(w_low_ready, 1)

            def swish(t, half, link):
                dve.wait_ge(bank_out[0][(RG * T + t) % 4], RG * T // 4 + 1)
                e, gate_in = (v[:, t, 256 * half:256 * half + 256] for v in (rg, o_ret))
                link(dve.tensor_scalar(e, e, 1.0, None, ALU.add))
                link(dve.reciprocal(e, e))
                link(dve.tensor_tensor(e, e, gate_in, ALU.mult))

            def gain_columns(ph, t):
                if t == 0:
                    dve.wait_ge(gain_loaded[ph], 16)
                for q in range(2):
                    dve.wait_ge(h_turned, 4 * ph + 2 * t + q + 1)
                    dve.tensor_tensor(hT[:, 4 * q:4 * q + 4, P * t:P * t + P],
                                      psum[2 * (1 - t) + q][:, :].rearrange("p (a s) -> p a s", a=4),
                                      gains[:, ph, 4 * q:4 * q + 4].unsqueeze(2).broadcast_to([P, 4, P]),
                                      ALU.mult).then_inc(hT_ready, 1)

            def rotate(l, s, link):
                j, t = divmod(s, T)
                dve.wait_ge(proj_done[l], s + 1)
                if s >= 3:
                    dve.wait_ge(rot_turned[l], s - 2)
                kind = "ret" if l == 0 and j == 2 else "rope"
                form = "p (h d x) -> p h d x" if kind == "ret" else "p (h x d) -> p h x d"

                def halves(ap, n):
                    v = ap.rearrange(form, h=n, x=2)
                    return (v[:, :, :, 0], v[:, :, :, 1]) if kind == "ret" else (v[:, :, 0, :], v[:, :, 1, :])

                cos = const(kind + "_cos", T, HEAD)[:, t, :]
                sin = const(kind + "_sin", T, HEAD)[:, t, :]
                bank = psum[s % 4][:, :]
                scale = rstd[:, t:t + 1]
                dve.scalar_tensor_tensor(out=rot[s % 3].rearrange("p (h d) -> p h d", h=8),
                                         in0=bank.rearrange("p (h d) -> p h d", h=8), scalar=scale,
                                         in1=cos.unsqueeze(1).broadcast_to([P, 8, HEAD]), op0=ALU.mult, op1=ALU.mult)
                src, dst, sn = halves(bank, 8), halves(rot_tmp, 8), halves(sin, 1)
                for a in range(2):
                    last = dve.scalar_tensor_tensor(out=dst[a], in0=src[1 - a], scalar=scale,
                                                    in1=sn[a].broadcast_to([P, 8, HEAD // 2]),
                                                    op0=ALU.mult, op1=ALU.mult)
                last.then_inc(bank_out[l][s % 4], 1)
                dve.wait_ge(bank_out[l][s % 4], s // 4 + 1)
                dve.tensor_tensor(rot[s % 3], rot[s % 3], rot_tmp, ALU.add).then_inc(rot_ready[l], 1)
                dve.wait_ge(rot_ready[l], s + 1)

            def head_max(l, m):
                i = n_ret[l] + m
                dve.wait_ge(s_done[l], i + 1)
                if m >= 4:
                    dve.wait_ge(p_turned[l], m - 3)
                elif l == 0:
                    dve.wait_ge(ret_done, m + 1)
                mask = const("mask0" if l == 0 else "mask1")
                for t, cols in ((0, slice(0, P)), (1, slice(P, 3 * P))):
                    last = dve.tensor_tensor_reduce(prob[i % 4][:, cols], psum[i % 2][:, cols], mask[:, cols],
                                                    -(HEAD ** -0.5), FAR, ALU.add, ALU.min, negm[:, m, t:t + 1])
                last.then_inc(s_out[l], 1)

            def head_sum(l, m, link):
                dve.wait_ge(exp_done[l], m + 1)
                if l == 1:
                    b, count = prob[m % 4], const("count1")
                    for t, cols in ((0, slice(0, P)), (1, slice(P, 3 * P))):
                        last = dve.tensor_tensor_reduce(b[:, cols], b[:, cols], count[:, cols],
                                                        1.0, 0.0, ALU.mult, ALU.add, den[:, m, t:t + 1])
                    link(last)
                dve.reciprocal(rden[:, m, 0:2], den[:, m, :])
                dve.reciprocal(rden[:, m, 2:3], den[:, m, 1:2]).then_inc(den_ready[l], 1)

            def decayed(n):
                dve.wait_ge(s_done[0], n + 1)
                dk = const("decay", RET, 2 * P)[:, n, :]
                dve.tensor_tensor(prob[n][:, 0:2 * P], psum[n % 2][:, 0:2 * P], dk, ALU.mult)
                dve.tensor_tensor(prob[n][:, 2 * P:3 * P], psum[n % 2][:, 2 * P:3 * P], dk[:, 0:P],
                                  ALU.mult).then_inc(ret_ready, 1)

            def retention_step(m, link):
                if m in (2, 3):
                    t = m - 2
                    if t == 0:
                        dve.wait_ge(ret_done, RET)
                    for n in range(RET):
                        last = dve.bn_stats(bnst[:, RET * t + n, :], psum[6 + t][:, P * n:P * n + P])
                    link(last)
                    for n in range(RET):
                        last = dve.bn_aggr(rstat[:, t, n, :], bnst[:, RET * t + n, :])
                    link(last)
                    if t:
                        dve.tensor_scalar(rvar.rearrange("p (t h) -> p t h", t=T), rstat[:, :, :, 1], EPS, None,
                                          ALU.add).then_inc(ret_var, 1)
                elif m == 5:
                    dve.wait_ge(ret_pow, 1)
                    step = small[:, 258:266]
                    link(dve.tensor_tensor(step, rrstd, rrstd, ALU.mult))
                    link(dve.tensor_tensor(step, step, rvar, ALU.mult))
                    link(dve.tensor_scalar(step, step, -0.5, 1.5, ALU.mult, ALU.add))
                    link(dve.tensor_tensor(rrstd, rrstd, step, ALU.mult))
                elif m in (6, 7):
                    t = m - 6
                    for n in range(RET):
                        at = RET * t + n
                        last = dve.tensor_scalar(o_ret[:, t, P * n:P * n + P], psum[6 + t][:, P * n:P * n + P],
                                                 rstat[:, t, n, 0:1], rrstd[:, at:at + 1], ALU.subtract, ALU.mult)
                    link(last)
                    dve.tensor_tensor(o_ret[:, t, :], o_ret[:, t, :], rg[:, t, :], ALU.mult).then_inc(ret_normed, 1)

            def route(l, t, link):
                dve.wait_ge(logits_done[l], t + 1)
                bank, bias = psum[4 + t], b_rt[:, l, :]
                for dst, cols in ((lg[:, t, 0:GROUPS], slice(0, GROUPS)), (lf[:, t, :], slice(GROUPS, 36))):
                    last = dve.scalar_tensor_tensor(out=dst, in0=bank[:, cols], scalar=rstd[:, t:t + 1],
                                                    in1=bias[:, cols], op0=ALU.mult, op1=ALU.add)
                link(last)
                link(dve.max(top[:, t, :], lg[:, t, :]))
                link(dve.max_index(idx_u[:, t, :], top[:, t, :], lg[:, t, :]))
                dve.tensor_scalar(gv[:, t:t + 1], top[:, t, 0:1], -1.0, None, ALU.mult)
                link(dve.tensor_copy(idx[:, t:t + 1], idx_u[:, t, 0:1]))
                link(dve.tensor_scalar(pen[:, t, :], const("iota")[:, 0:GROUPS], idx[:, t:t + 1], -FAR,
                                       ALU.not_equal, ALU.mult))
                by_group = "p (g e) -> p g e"
                link(dve.tensor_tensor(masked[:, t, :].rearrange(by_group, g=GROUPS),
                                       lf[:, t, :].rearrange(by_group, g=GROUPS),
                                       pen[:, t, :].unsqueeze(2).broadcast_to([P, GROUPS, 8]), ALU.add))
                best = top[:, T + t, :]
                link(dve.max(best, masked[:, t, :]))
                dve.tensor_tensor(gv[:, 6 + t:7 + t], best[:, 1:2], best[:, 0:1], ALU.subtract)\
                   .then_inc(gmax_ready[l], 1)
                link(dve.max_index(idx_u[:, T + t, :], best, masked[:, t, :]))
                pair = idx[:, 2 + 2 * t:4 + 2 * t]
                link(dve.tensor_copy(pair, idx_u[:, T + t, 0:2]))
                link(dve.tensor_tensor(chosen[:, t, :, :],
                                       const("iota")[:, 0:EXPERTS].unsqueeze(1).broadcast_to([P, 2, EXPERTS]),
                                       pair.unsqueeze(2).broadcast_to([P, 2, EXPERTS]), ALU.is_equal))
                dve.tensor_tensor(asg[:, t, :], chosen[:, t, 0, :], chosen[:, t, 1, :], ALU.add)\
                   .then_inc(assigned[l], 1)

            def places(l, link):
                dve.wait_ge(gexp_done[l], T)
                by = gv[:, 8:10]
                link(dve.scalar_tensor_tensor(out=by, in0=gv[:, 4:6], scalar=1.0, in1=gv[:, 2:4],
                                              op0=ALU.add, op1=ALU.mult))
                dve.reciprocal(by, by).then_inc(first_gates, 1)
                dve.wait_ge(counts_done[l], 1)
                link(dve.reduce_max(cnt[:, 0:1], psum[4][:, 0:32], AX.X))
                link(dve.tensor_scalar(limhit[:], const("limits"), cnt[:, 0:1], None, ALU.is_lt))
                link(dve.reduce_sum(cnt[:, 1:2], limhit[:], AX.X))
                dve.tensor_copy(rounds_i[:, l:l + 1], cnt[:, 1:2]).then_inc(rounds_ready[l], 1)
                dve.wait_ge(pos_done[l], 1)
                link(dve.scalar_tensor_tensor(out=posm[:, :, 0:EXPERTS],
                                              in0=psum[6][:, 0:64].rearrange("p (t e) -> p t e", t=T), scalar=1.0,
                                              in1=asg[:], op0=ALU.add, op1=ALU.mult))

            def experts_of(l, r, g, n, first_expert, base):
                chain = Chain(dve, dve_moe[l], base)
                no = group_no(r, g)
                cols = bass.ds(first_expert, n)
                slot_no = const("iota")[:, 1:1 + SLOTS]
                dve.tensor_tensor(
                    onehot[:, :, 0:n, :], slot_no.unsqueeze(1).unsqueeze(1).broadcast_to([P, T, n, SLOTS]),
                    posm[:, :, cols].unsqueeze(3).broadcast_to([P, T, n, SLOTS]), ALU.is_equal)\
                   .then_inc(onehot_ready[l], 1)
                dve.wait_ge(onehot_ready[l], no + 1)
                dve.wait_ge(gate_steps[l], GATE_STEPS)
                weight = gate[:, :, cols].unsqueeze(3).broadcast_to([P, T, n, SLOTS])
                if n == GE:
                    last = dve.tensor_tensor(gated[:], onehot[:], weight, ALU.mult)
                else:
                    for b in range(2):
                        last = dve.tensor_tensor(gated_twice[:, :, b, :, :], onehot[:, :, 0:n, :], weight, ALU.mult)
                last.then_inc(gated_ready[l], 1)
                for q in range(2):
                    dve.wait_ge(gathered[l], no * 2 + (q + 1))
                    dve.tensor_tensor(xT[:, 4 * q:4 * q + 4, 0:SLOTS * n],
                                      psum[q][:, 0:4 * SLOTS * n].rearrange("p (a s) -> p a s", a=4),
                                      gains[:, 2 * l + 1, 4 * q:4 * q + 4].unsqueeze(2).broadcast_to([P, 4, SLOTS * n]),
                                      ALU.mult).then_inc(xT_ready[l], 1)
                for k in range(n):
                    e = expert_no(r, g, k)
                    dve.wait_ge(gate_up_out[l], e + 1)
                    if k >= 2:
                        dve.wait_ge(hid_turned[l], e - 1)
                    eb, gb = eg[k % 2], gu[k % 2]
                    chain.link(dve.tensor_scalar(eb, eb, 1.0, None, ALU.add))
                    chain.link(dve.reciprocal(eb, eb))
                    chain.link(dve.tensor_tensor(eb, eb, gb[:, 0:P], ALU.mult))
                    dve.tensor_tensor(hid[k % 2], eb, gb[:, P:2 * P], ALU.mult).then_inc(hid_ready[l], 1)
                rows = y_rows(n)
                dve.wait_ge(down_done[l], down_no(r, g) + (1 if n == GE else 2))
                dve.tensor_copy(y_sb[0:rows, 512:1024], psum[7][0:rows, :]).then_inc(y_high[l], 1)
                for q in range(4):
                    half, t = divmod(q, 2)
                    dve.wait_ge(scattered[l], no * 4 + (q + 1))
                    hv = h[:, t, 512 * half:512 * half + 512]
                    dve.tensor_tensor(hv, hv, psum[q % 2][:, :], ALU.add).then_inc(added[l], 1)
                return chain.n

            dve.memset(work[:, 0:512], 0.0).then_inc(warm_ready, 1)
            norm_link(dve.memset(lg, -FAR))
            for l in range(LAYERS):
                link = Chain(dve, dve_attn[l]).link
                first_c = 2 if l else 0
                if l:
                    dve.wait_ge(gain_loaded[2 * l], 16)
                    split_chunks(l, 0, 0, first_c)
                for t in range(T):
                    split_columns(2 * l, t)
                dve.wait_ge(const_loaded[0], 16)
                for j in range(NW + 1):
                    if j < NW:
                        split_chunks(l, j, 0 if j else first_c, ROTATE_AT[0])
                    if j == 0:
                        for t in range(T):
                            variance(2 * l, t, 2 * t + 2 if l == 0 else 3 + t)
                        for t in range(T):
                            inverse_root(2 * l, t)
                    if 0 < j <= ROTATED[l]:
                        rotate(l, T * (j - 1), link)
                    swishing = l == 0 and RG < j <= RG + T
                    if swishing:
                        swish(j - RG - 1, 0, link)
                    if j < NW:
                        split_chunks(l, j, ROTATE_AT[0], ROTATE_AT[1])
                    if 0 < j <= ROTATED[l]:
                        rotate(l, T * (j - 1) + 1, link)
                    if swishing:
                        swish(j - RG - 1, 1, link)
                    if j < NW:
                        split_chunks(l, j, ROTATE_AT[1], C)
                if l == 0:
                    dve.wait_ge(const_loaded[1], 16)
                for n in range(n_ret[l]):
                    decayed(n)
                for m in range(HEADS[l] + 1):
                    if m < HEADS[l]:
                        head_max(l, m)
                    if m:
                        head_sum(l, m - 1, link)
                    if l == 0:
                        retention_step(m, link)
                route_link = Chain(dve, dve_route[l]).link

                def add_mixed(n, t):
                    dve.wait_ge(mixed[l], 2 * n + t + 1)
                    hv = h[:, t, 512 * n:512 * n + 512]
                    dve.tensor_tensor(hv, hv, mix_bank(n, t)[:, :], ALU.add).then_inc(mix_added[l], 1)

                for t in range(T):
                    add_mixed(0, t)
                for t in range(T):
                    add_mixed(1, t)
                    variance(2 * l + 1, t, 3 + t)
                    gain_columns(2 * l + 1, t)
                    inverse_root(2 * l + 1, t)
                    if t < T - 1:
                        scale_rows(t)
                    route(l, t, route_link)
                scale_rows(T - 1)
                places(l, route_link)

                def full_groups(r):
                    with dve.Fori(0, FULL) as g:
                        n = experts_of(l, r, g, GE, g * GE, r * DVE_ROUND + g * DVE_GROUP)
                        assert n == DVE_GROUP

                def last_group(r):
                    n = experts_of(l, r, FULL, TAIL, FULL * GE, r * DVE_ROUND + FULL * DVE_GROUP)
                    Chain(dve, dve_moe[l], r * DVE_ROUND + FULL * DVE_GROUP + n).link(
                        dve.tensor_scalar(posm[:, :, 0:EXPERTS], posm[:, :, 0:EXPERTS], -float(SLOTS), None, ALU.add))
                    assert FULL * DVE_GROUP + n + 1 == DVE_ROUND

                full_groups(0)
                dve.wait_ge(rounds_ready[l], 1)
                more = dve.value_load(rounds_i[0:1, l:l + 1], min_val=0, max_val=MAX_ROUNDS - 1)
                last_group(0)
                with dve.If(more > 0):
                    with dve.Fori(1, more + 1) as r:
                        full_groups(r)
                        last_group(r)

            for t in range(T):
                variance(2 * LAYERS, t, 3 + t)
            dve.wait_ge(fin_loaded, 16)
            for t in range(T):
                inverse_root(2 * LAYERS, t)
                dve.scalar_tensor_tensor(out=xn_t[:, t, :], in0=h[:, t, :], scalar=rstd[:, t:t + 1],
                                         in1=gain_row, op0=ALU.mult, op1=ALU.mult).then_inc(xn_ready, 1)


_INS = ['x', 'mix_norm_even', 'w_in_even', 'w_out_even', 'mix_norm_odd', 'w_in_odd', 'w_out_odd', 'ffn_norm',
        'w_router_group', 'b_router_group', 'w_router_expert', 'b_router_expert', 'w_expert_gate',
        'w_expert_up', 'w_expert_down', 'final_norm']


def kernel(**inputs):
    import concourse.bacc as _bacc
    from concourse.bass_utils import run_bass_kernel_spmd as _run

    nc = _bacc.Bacc("TRN2", target_bir_lowering=False, num_devices=1)
    arrays, args = {}, []
    for name in _INS:
        a = np.ascontiguousarray(inputs[name])
        arrays[f"in_{name}"] = a
        args.append(nc.dram_tensor(f"in_{name}", a.shape, mybir.dt.from_np(a.dtype), kind="ExternalInput").ap())
    arrays["shape_consts"] = shape_constants()
    args.append(nc.dram_tensor("shape_consts", (P, CONST_COLS), F32, kind="ExternalInput").ap())
    args.append(nc.dram_tensor("out_0", (1, SEQ, D), F32, kind="ExternalOutput").ap())
    build(nc, *args)
    r = _run(nc, [arrays], core_ids=[0])
    return r.results[0]["out_0"]
```
